# Optimizing a Trainium2 kernel written in Bass

```python
import jax, jax.numpy as jnp
from jax import lax
import numpy as np

D_MODEL = 1024
BATCH = 1
SEQ = 512
DEPTH = 2
DEC_BATCH = 8
DEC_SEQ = 16
PAST_LEN = 256

CHUNK = 64
D_CONV = 512
N_CONV_HEADS = 8
CONV_WIDTH = 3
D_POOL = 512
POOL_WINDOWS = (2, 4, 8, 16)
N_POOL_GROUPS = len(POOL_WINDOWS)
POOL_GROUP = D_POOL // N_POOL_GROUPS
POOL_STATE = max(POOL_WINDOWS) - 1
D_MIX = D_CONV + D_POOL
D_IN = 3 * D_CONV + D_POOL
D_FF = 2816
N_MEM = 256
N_XHEADS = 4
XHEAD_DIM = D_MODEL // N_XHEADS
EPS = 1e-6

kernel_name = "hybrid_conv_pool_streaming_encoder_step"

def rms_norm(x, g):
    xf = x.astype(jnp.float32)
    y = xf * lax.rsqrt(jnp.mean(xf * xf, axis=-1, keepdims=True) + EPS)
    return (y * g.astype(jnp.float32)).astype(x.dtype)

def swiglu_ffn(h, w_in, w_out):
    g, u = jnp.split(h @ w_in, 2, axis=-1)
    return (jax.nn.silu(g) * u) @ w_out

def short_conv(u, prefix, w):
    L = u.shape[1]
    full = jnp.concatenate([prefix.astype(u.dtype), u], axis=1)
    y = w[0] * full[:, 0:L]
    for k in range(1, CONV_WIDTH):
        y = y + w[k] * full[:, k:k + L]
    return y, full[:, -(CONV_WIDTH - 1):]

def multi_scale_pool(p, prefix, pos0):
    bsz, L, c = p.shape
    full = jnp.concatenate([prefix.astype(p.dtype), p], axis=1)
    cs = jnp.concatenate([jnp.zeros((bsz, 1, c), jnp.float32),
                          jnp.cumsum(full.astype(jnp.float32), axis=1)], axis=1)
    end = cs[:, POOL_STATE + 1:]
    pos = pos0 + jnp.arange(L)
    outs = []
    for g, w in enumerate(POOL_WINDOWS):
        sl = slice(g * POOL_GROUP, (g + 1) * POOL_GROUP)
        start = cs[:, POOL_STATE + 1 - w:POOL_STATE + 1 - w + L, sl]
        cnt = jnp.minimum(pos + 1, w).astype(jnp.float32)[None, :, None]
        outs.append((end[..., sl] - start) / cnt)
    mean = jnp.concatenate(outs, axis=-1)
    pooled = (mean - p.astype(jnp.float32)).astype(p.dtype)
    return pooled, full[:, -POOL_STATE:]

def token_mix(h, conv_prefix, pool_prefix, pos0, w_in, conv_w, pool_w, pool_scale, w_out):
    bsz, L, _ = h.shape
    z = h @ w_in
    b_gate, c_gate, v, p = jnp.split(z, [D_CONV, 2 * D_CONV, 3 * D_CONV], axis=-1)
    conv_y, conv_state = short_conv(c_gate * v, conv_prefix, conv_w)
    y_a = b_gate * conv_y
    pooled, pool_state = multi_scale_pool(p, pool_prefix, pos0)
    y_b = jnp.einsum('blgc,gcd->blgd', pooled.reshape(bsz, L, N_POOL_GROUPS, POOL_GROUP), pool_w)
    y_b = y_b.reshape(bsz, L, D_POOL) * pool_scale
    out = jnp.concatenate([y_a, y_b], axis=-1) @ w_out
    return out, conv_state, pool_state

def mem_kv(mem, g, w_kv):
    bsz = mem.shape[0]
    k, v = jnp.split(rms_norm(mem, g) @ w_kv, 2, axis=-1)
    return (k.reshape(bsz, N_MEM, N_XHEADS, XHEAD_DIM), v.reshape(bsz, N_MEM, N_XHEADS, XHEAD_DIM))

def cross_attend(h, k, v, wq, wo):
    bsz, L, _ = h.shape
    q = (h @ wq).reshape(bsz, L, N_XHEADS, XHEAD_DIM)
    s = jnp.einsum('blhd,bmhd->bhlm', q, k.astype(q.dtype)).astype(jnp.float32) * (XHEAD_DIM ** -0.5)
    pr = jax.nn.softmax(s, axis=-1).astype(h.dtype)
    o = jnp.einsum('bhlm,bmhd->blhd', pr, v.astype(h.dtype)).reshape(bsz, L, D_MODEL)
    return o @ wo

def setup_inputs(seed: int = 0) -> dict:
    key = jax.random.key(seed)
    ks = jax.random.split(key, 24)
    nrm = lambda k, shape, s: jax.random.normal(k, shape, jnp.float32) * s
    return {
        "x_prompt": nrm(ks[0], (BATCH, SEQ, D_MODEL), 1.0),
        "x_sample": nrm(ks[1], (DEC_BATCH, DEC_SEQ, D_MODEL), 1.0),
        "mem_prompt": nrm(ks[2], (BATCH, N_MEM, D_MODEL), 1.0),
        "cache_mem_k": nrm(ks[3], (DEPTH, DEC_BATCH, N_MEM, N_XHEADS, XHEAD_DIM), 1.0),
        "cache_mem_v": nrm(ks[4], (DEPTH, DEC_BATCH, N_MEM, N_XHEADS, XHEAD_DIM), 1.0),
        "state_conv": nrm(ks[5], (DEPTH, DEC_BATCH, CONV_WIDTH - 1, D_CONV), 1.0),
        "state_pool": nrm(ks[6], (DEPTH, DEC_BATCH, POOL_STATE, D_POOL), 1.0),
        "ffn_norm": 1.0 + nrm(ks[7], (DEPTH, 2, D_MODEL), 0.05),
        "ffn_w_in": nrm(ks[8], (DEPTH, 2, D_MODEL, 2 * D_FF), D_MODEL ** -0.5),
        "ffn_w_out": nrm(ks[9], (DEPTH, 2, D_FF, D_MODEL), D_FF ** -0.5),
        "mix_norm": 1.0 + nrm(ks[10], (DEPTH, D_MODEL), 0.05),
        "mix_w_in": nrm(ks[11], (DEPTH, D_MODEL, D_IN), D_MODEL ** -0.5),
        "conv_w": nrm(ks[12], (DEPTH, CONV_WIDTH, D_CONV), CONV_WIDTH ** -0.5),
        "pool_w": nrm(ks[13], (DEPTH, N_POOL_GROUPS, POOL_GROUP, POOL_GROUP), POOL_GROUP ** -0.5),
        "pool_scale": 1.0 + nrm(ks[14], (DEPTH, D_POOL), 0.05),
        "mix_w_out": nrm(ks[15], (DEPTH, D_MIX, D_MODEL), D_MIX ** -0.5),
        "xattn_norm": 1.0 + nrm(ks[16], (DEPTH, D_MODEL), 0.05),
        "mem_norm": 1.0 + nrm(ks[17], (DEPTH, D_MODEL), 0.05),
        "xattn_wq": nrm(ks[18], (DEPTH, D_MODEL, D_MODEL), D_MODEL ** -0.5),
        "xattn_wkv": nrm(ks[19], (DEPTH, D_MODEL, 2 * D_MODEL), D_MODEL ** -0.5),
        "xattn_wo": nrm(ks[20], (DEPTH, D_MODEL, D_MODEL), D_MODEL ** -0.5),
        "final_norm": 1.0 + nrm(ks[21], (D_MODEL,), 0.05),
    }

def reference(x_prompt, x_sample, mem_prompt, cache_mem_k, cache_mem_v, state_conv, state_pool,
              ffn_norm, ffn_w_in, ffn_w_out, mix_norm, mix_w_in, conv_w, pool_w, pool_scale, mix_w_out,
              xattn_norm, mem_norm, xattn_wq, xattn_wkv, xattn_wo, final_norm):
    def layer(x, l, conv_prefix, pool_prefix, pos0, mk, mv):
        x = x + 0.5 * swiglu_ffn(rms_norm(x, ffn_norm[l, 0]), ffn_w_in[l, 0], ffn_w_out[l, 0])
        mix, conv_state, pool_state = token_mix(rms_norm(x, mix_norm[l]), conv_prefix, pool_prefix, pos0,
                                                mix_w_in[l], conv_w[l], pool_w[l], pool_scale[l], mix_w_out[l])
        x = x + mix
        x = x + cross_attend(rms_norm(x, xattn_norm[l]), mk, mv, xattn_wq[l], xattn_wo[l])
        x = x + 0.5 * swiglu_ffn(rms_norm(x, ffn_norm[l, 1]), ffn_w_in[l, 1], ffn_w_out[l, 1])
        return x, conv_state, pool_state

    bp = x_prompt.shape[0]
    zero_conv = jnp.zeros((bp, CONV_WIDTH - 1, D_CONV), x_prompt.dtype)
    zero_pool = jnp.zeros((bp, POOL_STATE, D_POOL), x_prompt.dtype)
    xp = x_prompt
    mk_p, mv_p, conv_p, pool_p = [], [], [], []
    for l in range(DEPTH):
        mk, mv = mem_kv(mem_prompt, mem_norm[l], xattn_wkv[l])
        xp, cst, pst = layer(xp, l, zero_conv, zero_pool, 0, mk, mv)
        mk_p.append(mk); mv_p.append(mv); conv_p.append(cst); pool_p.append(pst)
    y_prompt = rms_norm(xp, final_norm)

    xs = x_sample
    conv_s, pool_s = [], []
    for l in range(DEPTH):
        xs, cst, pst = layer(xs, l, state_conv[l], state_pool[l], PAST_LEN, cache_mem_k[l], cache_mem_v[l])
        conv_s.append(cst); pool_s.append(pst)
    y_sample = rms_norm(xs, final_norm)

    mem_k_prompt = jnp.stack(mk_p)
    mem_v_prompt = jnp.stack(mv_p)
    conv_state_prompt = jnp.stack(conv_p)
    pool_state_prompt = jnp.stack(pool_p)
    conv_state_sample = jnp.stack(conv_s)
    pool_state_sample = jnp.stack(pool_s)
    return (y_prompt, y_sample, mem_k_prompt, mem_v_prompt, conv_state_prompt, pool_state_prompt,
            conv_state_sample, pool_state_sample)


_drawn_inputs = setup_inputs


def setup_inputs(seed=0):
    import zlib

    import numpy as np

    out = dict(_drawn_inputs(seed))
    spreads = {}
    factors = {'xattn_norm': 8.0}
    for name, (base, spread) in spreads.items():
        noise = np.random.default_rng([zlib.crc32(name.encode()), seed]).standard_normal(out[name].shape)
        drawn = base * np.exp(spread * noise) if base else spread * noise
        out[name] = __import__('jax').numpy.asarray(drawn.astype(out[name].dtype))
    for name, factor in factors.items():
        out[name] = (out[name] * factor).astype(out[name].dtype)
    return out
```

```python
import concourse.bass as bass
from concourse import mybir
from contextlib import ExitStack

D = 1024
P = 128
DEPTH = 2
TP, NB, TD = 512, 8, 16
T = TP + NB * TD
HT = T // 2
DC = 512
DFF = 2816
NMEM = 256
NH = 4
CW = 3
PS = 15
EPS = 1e-6
KC = D // P
GROUPS = (8, 8, 6)
GSTART = (0, 8, 16)

G_FFN = (0, 24)
G_MIX, G_ATT, G_MEM, G_PSCALE, G_CONV = 8, 16, 32, 40, 44
G_LAYER = 56
G_NEXT = G_LAYER

N_FFN = 69
FFN_IN = (1, 25, 49)
FFN_OUT = (17, 41, 61)
M_P, M_SP = (2, 3, 4, 6), (5, 8)
M_C, M_V, M_B = (7, 9, 19, 20), (10, 11, 21, 22), (14, 16, 23, 25)
M_PW, M_SC = (12, 13, 17, 18), (15, 24)
M_OUT = 26
N_MIX = 34
A_Q = 1
A_KB, A_TK = (9, 10, 12, 14), (11, 13, 15, 17)
A_VB, A_S, A_TP, A_PV = (16, 19, 21, 22), (18, 20, 24, 27), (23, 26, 29, 31), (25, 28, 30, 32)
A_WO = 33
N_ATT = 41
I_FFN = (0, N_FFN + N_MIX + N_ATT)
I_MIX, I_ATT = N_FFN, N_FFN + N_MIX
N_LAYER = 2 * N_FFN + N_MIX + N_ATT
SHIFT = -N_LAYER % 4
N_PRO = 8
MIX_STEPS = [("P", 0), ("P", 1), ("P", 2), ("p", 0), ("P", 3), ("C", 0), ("p", 1), ("C", 1), ("V", 0), ("V", 1),
             ("W", 0), ("W", 1), ("B", 0), ("c", 0), ("B", 1), ("W", 2), ("W", 3), ("C", 2), ("C", 3), ("V", 2),
             ("V", 3), ("B", 2), ("c", 1), ("B", 3)]
ATT_STEPS = [("K", 0), ("K", 1), ("k", 0), ("K", 2), ("k", 1), ("K", 3), ("k", 2), ("V", 0), ("k", 3), ("S", 0),
             ("s", 0), ("V", 1), ("S", 1), ("s", 1), ("V", 2), ("V", 3), ("T", 0), ("S", 2), ("O", 0), ("T", 1),
             ("s", 2), ("S", 3), ("O", 1), ("T", 2), ("s", 3), ("O", 2), ("T", 3), ("O", 3)]
HID_Q = 38

H_FFN0, H_MIX, H_Q, H_KV, H_WO, H_FFN1 = 0, 68, 92, 100, 116, 124
GROW_A_STEP, GROW_V_STEP = 16, 115

GROW_IN = dict(item_ready=4, item_done=4, w_hi=4, w_ready=4, raw_full0=16, raw_full1=16, gate_silu=2,
               hid_f32=2, hid_hi=2, hid_ready=2)
GROW_OUT = dict(item_ready=4, item_done=4, w_hi=4, w_ready=4, raw_full0=16, raw_full1=16)
GROW_BLOCKS = dict(w_ready=4, raw_full0=16, raw_full1=16)
GROW_PAIR = dict(k_turned=4, k_copied=4, scores_done=4, q_placed=1, nmax_dec=1, dec_exp=1, p_scaled=1, p_turned=1, p_placed=1,
                 raw_used=2, o_copied=1, o_turned=1, o_hi=1, o_placed=1, raw_full0=32, raw_full1=32, a_step=1,
                 v_step=5)
GROW_LAYER = dict(item_ready=N_LAYER, item_done=N_LAYER, w_hi=192, w_ready=192, raw_full0=56 * 16,
                  raw_full1=56 * 16, gate_silu=44, hid_f32=52, hid_hi=60, hid_ready=60, xn_hi=32, x_sq=32,
                  xn_ready=32, sq_added=28, recip_done=4, rstd_ready=4, par_ready=1, misc_loaded=48, pw_hi=1,
                  pw_ready=1, part_hi=28, memx_ready=8, exp_done=4, prob_ready=4, stage_free=4, k_sent=8, dec_zeroed=2,
                  k_turned=16, k_copied=16, scores_done=16, q_placed=4, dec_exp=4, p_scaled=4, p_turned=4,
                  p_placed=4, raw_used=8, o_copied=4, o_turned=4, o_hi=4, o_placed=4, a_step=GROW_A_STEP,
                  v_step=GROW_V_STEP, stage_sent=64 * (NB + 1), kv_sent=128, nmax_ready=4, nmax_dec=4)


PARAM_LOADS = 7 * DEPTH + 1


class Counts:

    def __init__(self, eng, sems, settled, settles=False):
        self.settled = settled
        self.eng, self.sems, self.n, self.turns, self.last, self.settles = eng, sems, {}, [], None, settles

    def value(self, name, more=0):
        v = self.n.get(name, 0) + more
        for i, grow in self.turns:
            if grow.get(name, 0):
                v = i * grow[name] + v
        return v

    def take(self, name, n=1):
        self.n[name] = self.n.get(name, 0) + n
        self.eng.wait_ge(self.sems[name], self.value(name))
        if self.settles:
            self.settle()

    def settle(self):
        self.eng.sem_inc(self.settled, 1)

    def note(self, name, n=1):
        self.n[name] = self.n.get(name, 0) + n

    def did(self, name):
        self.note(name)
        self.last = name

    def own(self):
        if self.last:
            self.eng.wait_ge(self.sems[self.last], self.value(self.last))

    def loop(self, lo, hi, grow):
        return Turns(self, lo, hi, grow)


class Turns:

    def __init__(self, counts, lo, hi, grow):
        self.c, self.lo, self.hi, self.grow = counts, lo, hi, grow

    def __enter__(self):
        self.c.own()
        self.c.last = None
        self.c.settle()
        self.f = self.c.eng.Fori(self.lo, self.hi)
        i = self.f.__enter__()
        self.start = dict(self.c.n)
        if self.lo:
            for name, n in self.grow.items():
                self.c.n[name] = self.c.n.get(name, 0) - self.lo * n
        self.inside = dict(self.c.n)
        self.c.turns.append((i, self.grow))
        return i

    def __exit__(self, *error):
        if error[0]:
            return False
        self.c.own()
        self.c.last = None
        grown = {k: v - self.inside.get(k, 0) for k, v in self.c.n.items() if v != self.inside.get(k, 0)}
        wrong = {k: v for k, v in grown.items() if v != self.grow.get(k, 0)}
        assert not wrong, f"{self.c.eng.engine}: grown {wrong}"
        self.c.turns.pop()
        self.f.__exit__(None, None, None)
        self.c.n = {**self.start, **{k: self.start.get(k, 0) + (self.hi - self.lo) * v for k, v in grown.items()}}


def program(nc, x_prompt, x_sample, mem_prompt, cache_k, cache_v, state_conv, state_pool, ffn_norm,
            ffn_w_in, ffn_w_out, mix_norm, mix_w_in, conv_w, pool_w, pool_scale, mix_w_out,
            xattn_norm, mem_norm, wq, wkv, wo, final_norm,
            y_prompt, y_sample, mem_k_out, mem_v_out, conv_p_out, pool_p_out, conv_s_out, pool_s_out):
    f32, f32r = mybir.dt.float32, mybir.dt.float32r
    ALU, ACT, AX = mybir.AluOpType, mybir.ActivationFunctionType, mybir.AxisListType
    ds = bass.ds

    ctx = ExitStack()
    with ctx:
        def sb(name, shape, dt=f32):
            return ctx.enter_context(nc.sbuf_tensor(name, shape, dt))

        xT = sb("xT", [P, KC, T])
        X = sb("X", [P, 2, KC, T], f32r)
        Xflat = X[:, :, :, :].rearrange("p a k t -> p (a k t)")
        H = sb("H", [P, 2, KC, T], f32r)
        Hf = H[:, :, :, :].bitcast(f32)
        raw = sb("raw", [P, 2, 2048])
        W = sb("W", [P, 2, 4, 1024], f32r)
        Mr = sb("Mr", [P, 2048], f32r)
        Mf = sb("Mf", [P, 7040])
        memT = sb("memT", [P, KC, NMEM])
        sqsum = sb("sqsum", [P, T])
        rstd = sb("rstd", [P, T])
        mrow = sb("mrow", [P, 3, DC])
        stage = sb("stage", [P, 3, 256])
        ident = sb("ident", [P, P])
        onesd = sb("onesd", [P, P])
        par = sb("par", [P, 120])
        parl = sb("parl", [P, 64])
        invc = sb("invc", [P, 16])
        small = sb("small", [P, 48])
        psum = ctx.enter_context(nc.psum_tensor("psum", [P, 4096], f32))

        tmp = [Mf[:, i * T:(i + 1) * T] for i in range(4)]
        gate, val, sq = tmp[0:2], tmp[2:4], tmp[0:2]
        PX = PS + TP + NB * (PS + 16)
        UX = 2 + TP + NB * 18
        p_ext = [Mf[:, 2580 + i * 776:2580 + i * 776 + PX] for i in range(2)]
        u_ext = [Mf[:, 4132 + i * UX:4132 + (i + 1) * UX] for i in range(2)]
        sums = [Mf[:, 0:PX], Mf[:, 4132:4132 + PX]]
        pfx_pool = Mf[:, 5448:5928].rearrange("p (g b t) -> p g b t", g=4, t=PS)
        pfx_conv = Mf[:, 5928:5992].rearrange("p (g b t) -> p g b t", g=4, t=2)
        kv_st = [Mf[:, 2560 + i * 512:2560 + (i + 1) * 512].rearrange("p (c f) -> p c f", c=2) for i in range(4)]
        prob = [Mf[:, 4608 + i * 1024:4608 + (i + 1) * 1024].rearrange("p (t m) -> p t m", t=4) for i in range(2)]
        qblk, pblk = Mf[:, 0:2176], Mf[:, 2176:4352]
        k_dec = [Mf[:, 4352 + i * 1024:4352 + (i + 1) * 1024] for i in range(2)]
        p_dec, o_dec = Mf[:, 6400:6656], Mf[:, 6656:6912]
        KTp = Xflat[:, 0:4096].rearrange("p (a k m) -> p a k m", a=2, k=KC)
        memx = Xflat[:, 4096:8192].rearrange("p (a k m) -> p a k m", a=2, k=KC)
        PT = Xflat[:, 6144:8192].rearrange("p (a c t) -> p a c t", a=2, c=2)
        Vp = [Xflat[:, 8192:10240].rearrange("p (c f) -> p c f", c=2), Mr[:, :].rearrange("p (c f) -> p c f", c=2)]
        pw = Mr[:, 0:1024].rearrange("p (a g f) -> p a g f", a=2, g=4)

        names = """x_loaded mem_loaded rows_loaded misc_loaded consts raw_full0 raw_full1 w_hi w_ready item_ready
            item_done mem_sq mem_ms mem_rstd xn_hi x_sq xn_ready sq_added recip_done rstd_ready gate_silu hid_f32
            hid_hi hid_ready par_ready pw_hi pw_ready part_hi memx_ready exp_done prob_ready nmax_ready nmax_dec mem_scaled settled_sp settled_pool settled_act settled_dve settled_pe stage_free stage_sent
            kv_sent k_sent dec_zeroed k_turned k_copied scores_done q_placed dec_exp p_scaled p_turned p_placed
            raw_used o_copied o_turned o_hi o_placed a_step v_step y_made y_copied y_sent""".split()
        S = {n: ctx.enter_context(nc.semaphore(n)) for n in names}

        def slot_of(n):
            return (n + N_PRO + (SHIFT if n >= I_ATT + A_WO else 0)) % 4

        def bank(s, b, lo=0, hi=512):
            return psum[:, (2 * s + b) * 512 + lo:(2 * s + b) * 512 + hi]

        def slot(s):
            return psum[:, s * 1024:(s + 1) * 1024]

        def tok(s):
            return slot(s).rearrange("p (b t) -> p b t", b=2)[:, :, 0:HT]

        def two(ap):
            return ap.rearrange("p (b t) -> p b t", b=2)

        def samples(ap, off, n):
            return ap[:, off:off + NB * n].rearrange("p (b t) -> p b t", b=NB)

        def diag(blk, c):
            return blk[:, c * 1024:c * 1024 + 1152].rearrange("p (e s) -> p e s", s=144)[:, :, 0:16]

        def raw_half(h):
            return raw[:, (h // 2) % 2, :].rearrange("p (k n) -> p k n", n=256)[:, :, (h % 2) * P:(h % 2 + 1) * P]

        def w_half(a, h):
            return W[:, a, h % 4, :].rearrange("p (k n) -> p k n", n=P)

        def done_value(l, n):
            return l * N_LAYER + (N_PRO + n + 1)

        def hidden(a, q):
            return H[:, a, q, :] if isinstance(q, int) else H[:, a, ds(q, 1), :].rearrange("p a t -> p (a t)")

        def dec_cols(a, c, n):
            return (a[:, :, TP + n * 32:TP + (n + 1) * 32] if isinstance(n, int) else a[:, :, ds(n * 32 + TP, 32)])\
                .rearrange("p (h c) (b t) -> p c b h t", c=2, b=2)[:, c]

        block = ctx.enter_context(nc.Block())

        @block.sync
        def _(sp):
            c = Counts(sp, S, S["settled_sp"], True)
            for t in range(5):
                src = x_prompt[0, t * P:(t + 1) * P, :] if t < 4 else x_sample.rearrange("b t d -> (b t) d")
                sp.dma_start(Mf[:, t * D:(t + 1) * D], src).then_inc(S["x_loaded"], 16)

            def load(u, ap, k=KC):
                sp.dma_start(raw[:, u, 0:k * 256].rearrange("p (k n) -> p k n", n=256),
                             ap.rearrange("a (k p) n -> p (a k) n", p=P)).then_inc(S[f"raw_full{u}"], 16)
                c.note(f"raw_full{u}", 16)

            def freed():
                c.take("w_ready", 2)

            def w_in(l, w, col):
                return ffn_w_in[ds(l, 1), w, :, ds(col, 256)]

            load(0, w_in(0, 0, 0))
            load(1, w_in(0, 0, DFF))
            sp.wait_ge(S["item_ready"], 6)
            sp.dma_start(Mf[:, 2 * D:4 * D].rearrange("p (c d) -> p c d", c=2),
                         mem_prompt[0].rearrange("(c p) d -> p c d", p=P)).then_inc(S["mem_loaded"], 16)

            def ffn_loads(l, w):
                for g, (k, g0) in enumerate(zip(GROUPS, GSTART)):
                    with c.loop(1 if w == 0 and g == 0 else 0, k // 2, GROW_BLOCKS) as i:
                        for u in range(2):
                            freed()
                            load(u, w_in(l, w, i * 256 + (g0 * P + u * DFF)))
                    with c.loop(0, 2, GROW_BLOCKS) as i:
                        for u in range(2):
                            freed()
                            load(u, ffn_w_out[ds(l, 1), w, g0 * P:(g0 + k) * P, ds(i * 512 + u * 256, 256)], k)

            def matrix_loads(l, m, pairs):
                with c.loop(0, pairs, GROW_BLOCKS) as i:
                    for u in range(2):
                        freed()
                        load(u, m[ds(l, 1), :, ds(i * 512 + u * 256, 256)])

            def cached(cache, l, b, u):
                sp.dma_start(raw[:, u, :].rearrange("p (c d) -> p c d", c=2),
                             cache[ds(l, 1), ds(b, 1), :, :, :].rearrange("a b (c p) h d -> p (a b c) (h d)", p=P))\
                    .then_inc(S[f"raw_full{u}"], 16)
                c.note(f"raw_full{u}", 16)

            with c.loop(0, DEPTH, GROW_LAYER) as l:
                ffn_loads(l, 0)
                for n, col in enumerate((6, 7, 2, 4, 0, 3, 5, 1)):
                    freed()
                    load(n % 2, mix_w_in[ds(l, 1), :, col * 256:(col + 1) * 256])
                matrix_loads(l, mix_w_out, 2)
                matrix_loads(l, wq, 2)
                matrix_loads(l, wkv, 4)
                for u in range(2):
                    freed()
                    load(u, wo[ds(l, 1), :, u * 256:(u + 1) * 256])
                for u in range(2):
                    freed()
                    cached(cache_k, l, u, u)
                for u in range(2):
                    c.take("k_turned", 2)
                    cached(cache_k, l, 2 + u, u)
                with c.loop(0, 2, GROW_PAIR) as n:
                    for u in range(2):
                        c.take("k_turned", 2)
                        cached(cache_v, l, n * 2 + u, u)
                    for u in range(2):
                        c.take("raw_used")
                        cached(cache_k, l, n * 2 + (4 + u), u)
                for u in range(2):
                    c.take("k_turned", 2)
                    cached(cache_v, l, 4 + u, u)
                for u in range(2):
                    c.take("raw_used")
                    cached(cache_v, l, 6 + u, u)
                for u in range(2):
                    c.take("raw_used")
                    load(u, wo[ds(l, 1), :, (2 + u) * 256:(3 + u) * 256])
                ffn_loads(l, 1)
                for u in range(2):
                    freed()
                    load(u, w_in(1 - l, 0, u * DFF))

        @block.gpsimd
        def _(pool):
            c = Counts(pool, S, S["settled_pool"], True)
            nc.gpsimd.memset(ident[:, :], 0.0).then_inc(S["consts"], 1)
            nc.gpsimd.memset(onesd[:, :], 1.0 / D).then_inc(S["consts"], 1)
            for t in range(PS):
                nc.gpsimd.memset(invc[:, t:t + 1], 1.0 / (t + 1)).then_inc(S["consts"], 1)
            pool.wait_ge(S["consts"], 2 + PS)
            nc.gpsimd.affine_select(out=ident[:, :], in_=ident[:, :], compare_op=ALU.not_equal, fill=1.0,
                                    base=0, pattern=[[-1, P]], channel_multiplier=1).then_inc(S["consts"], 1)
            pool.sem_inc(S["stage_free"], 1)

            def sent(l, n, s_out, p_out, col, rows):
                def end(b):
                    return (b % 4 + 1) * (rows + 16)

                pool.wait_ge(S["item_done"], done_value(l, n))
                c.settle()
                for b in range(NB):
                    pool.dma_start(s_out[ds(l, 1), b, :, col:col + 256].rearrange("a t f -> (a t) f"),
                                   stage[end(b) - rows:end(b), b // 4, :]).then_inc(S["stage_sent"], 16)
                pool.dma_start(p_out[ds(l, 1), :, :, col:col + 256].rearrange("a b t f -> (a b t) f"),
                               stage[16 - rows:16, 2, :]).then_inc(S["stage_sent"], 16)
                c.take("stage_sent", 16 * (NB + 1))
                pool.sem_inc(S["stage_free"], 1)

            with c.loop(0, DEPTH, GROW_LAYER) as l:
                for j in range(2):
                    sent(l, I_MIX + M_SP[j], pool_s_out, pool_p_out, j * 256, PS)
                for j in range(2):
                    sent(l, I_MIX + M_SC[j], conv_s_out, conv_p_out, j * 256, 2)
                pool.wait_ge(S["hid_ready"], l * GROW_LAYER["hid_ready"] + HID_Q)
                c.settle()
                nc.gpsimd.memset(qblk, 0.0).then_inc(S["dec_zeroed"], 1)
                for items, out, i0 in ((A_KB, mem_k_out, 0), (A_VB, mem_v_out, 2)):
                    for h in range(NH):
                        pool.wait_ge(S["item_done"], done_value(l, I_ATT + items[h]))
                        c.settle()
                        pool.dma_start(out[ds(l, 1), 0, :, h, :].rearrange("a (c p) d -> p (a c) d", p=P),
                                       kv_st[i0 + h % 2]).then_inc(S["kv_sent"], 16)
                        c.take("kv_sent", 16)
                        pool.sem_inc(S["k_sent"], 1)
                nc.gpsimd.memset(pblk, 0.0).then_inc(S["dec_zeroed"], 1)

        @block.scalar
        def _(act):
            c = Counts(act, S, S["settled_act"])

            def split(h):
                if h % 2 == 0:
                    c.take(f"raw_full{(h // 2) % 2}", 16)
                c.own()
                nc.scalar.activation(w_half(0, h), raw_half(h), ACT.Copy).then_inc(S["w_hi"], 1)
                c.did("w_hi")

            def norm_part(m, gcol):
                c.own()
                nc.scalar.activation(X[:, 0, m, :], xT[:, m, :], ACT.Copy, scale=parl[:, gcol + m:gcol + m + 1])\
                    .then_inc(S["xn_hi"], 1)
                c.did("xn_hi")
                c.own()
                nc.scalar.activation(sqsum[:, :] if m == 0 else sq[m % 2], xT[:, m, :], ACT.Square)\
                    .then_inc(S["x_sq"], 1)
                c.did("x_sq")

            def rms():
                c.take("item_ready")
                c.note("item_done")
                c.take("recip_done")
                c.own()
                nc.scalar.activation(rstd[:, :], sqsum[:, :], ACT.Sqrt).then_inc(S["rstd_ready"], 1)
                c.did("rstd_ready")

            def hidden_hi(out, v):
                c.take("hid_f32")
                c.own()
                nc.scalar.activation(out, v, ACT.Copy).then_inc(S["hid_hi"], 1)
                c.did("hid_hi")

            for r0, src in parameter_rows(ffn_norm, mix_norm, xattn_norm, mem_norm, pool_scale, conv_w, final_norm):
                act.dma_start(mrow[r0:r0 + src.shape[0], 0, 0:P], src).then_inc(S["rows_loaded"], 16)
            for h in range(4):
                split(h)
            c.note("item_ready", 6)
            c.take("item_done", 6)
            c.take("par_ready")
            for m in range(KC):
                if m >= 3:
                    act.wait_ge(S["sq_added"], m - 2)
                norm_part(m, 0)
            act.wait_ge(S["mem_loaded"], 16)
            for i in range(2):
                c.own()
                nc.scalar.activation(Mf[:, (4 + i) * D:(5 + i) * D], Mf[:, (2 + i) * D:(3 + i) * D], ACT.Square,
                                     accum_out=small[:, i:i + 1]).then_inc(S["mem_sq"], 1)
                c.did("mem_sq")
            act.wait_ge(S["mem_ms"], 1)
            c.own()
            nc.scalar.activation(small[:, 2:4], small[:, 2:4], ACT.Sqrt).then_inc(S["mem_rstd"], 1)
            c.did("mem_rstd")
            c.note("item_ready", 2)
            c.note("item_done", 2)

            def gate_up(q, h0, first):
                for e in range(2):
                    c.take("item_ready")
                    if first and e == 0:
                        rms()
                    c.take("item_done")
                    c.own()
                    nc.scalar.activation(gate[e], gate[e], ACT.Silu).then_inc(S["gate_silu"], 1)
                    c.did("gate_silu")
                    split(h0 + 4 + e)
                for e in range(2):
                    c.take("item_ready")
                    c.note("item_done")
                    hidden_hi(hidden(0, q(e)), val[e])
                    split(h0 + 6 + e)

            def update(m, h, gcol=None):
                c.take("item_ready")
                c.take("item_done")
                if gcol is not None:
                    norm_part(m, gcol)
                split(h + 4)

            def ffn(w):
                h = (H_FFN0, H_FFN1)[w]
                for g, k in enumerate(GROUPS):
                    n = k // 2
                    if g == 0:
                        gate_up(lambda e: e, h, True)
                        n, h = n - 1, h + 4
                    with c.loop(0, n, GROW_IN) as i:
                        gate_up(lambda e: i * 2 + (2 * (g == 0) + e), h, False)
                    h += 4 * n
                    if g < 2:
                        with c.loop(0, 2, GROW_OUT) as i:
                            for m in range(4):
                                update(None, h + m)
                    else:
                        for m in range(KC):
                            update(m, h + m, (G_MIX, G_NEXT)[w])
                    h += KC

            with c.loop(0, DEPTH, GROW_LAYER) as l:
                c.own()
                act.dma_start(mrow[:, 0, :].rearrange("p (g d) -> p g d", g=4),
                              pool_w[ds(l, 1)].rearrange("a g c d -> c (a g) d")).then_inc(S["misc_loaded"], 16)
                act.dma_start(mrow[0:NB * PS, 1, :], state_pool[ds(l, 1)].rearrange("a b t f -> (a b t) f"))\
                    .then_inc(S["misc_loaded"], 16)
                act.dma_start(mrow[0:NB * 2, 2, :], state_conv[ds(l, 1)].rearrange("a b t f -> (a b t) f"))\
                    .then_inc(S["misc_loaded"], 16)
                c.take("par_ready")
                ffn(0)

                c.take("misc_loaded", 48)
                c.own()
                nc.scalar.activation(pw[:, 0, :, :], mrow[:, 0, :].rearrange("p (g f) -> p g f", g=4), ACT.Copy)\
                    .then_inc(S["pw_hi"], 1)
                c.did("pw_hi")
                c.take("item_ready")
                c.note("item_done")
                h = H_MIX
                for kind, e in MIX_STEPS:
                    c.take("item_ready")
                    if (kind, e) == ("P", 0):
                        rms()
                    n = I_MIX + (M_PW[e] if kind == "W" else 0)
                    if kind == "W":
                        c.own()
                        nc.scalar.activation(two(H[:, 0, 4 + e, :]), tok(slot_of(n)), ACT.Copy,
                                             scale=parl[:, G_PSCALE + e:G_PSCALE + e + 1]).then_inc(S["part_hi"], 1)
                        c.did("part_hi")
                    c.note("item_done")
                    if kind == "P":
                        hidden_hi(H[:, 0, 4 + e, :], val[e % 2])
                    if kind == "B":
                        hidden_hi(H[:, 0, e, :], val[e % 2])
                    if kind in "PCVB":
                        split(h + 4)
                        h += 1
                for m in range(KC):
                    update(m, h + m, G_ATT)

                for m in range(KC):
                    c.take("item_ready")
                    if m == 0:
                        rms()
                    c.take("item_done")
                    c.own()
                    nc.scalar.activation(H[:, 0, m, :], val[m % 2], ACT.Copy).then_inc(S["hid_hi"], 1)
                    c.did("hid_hi")
                    split(H_Q + 4 + m)
                for k in range(KC):
                    c.own()
                    nc.scalar.activation(memx[:, 0, k, :], memT[:, k, :], ACT.Copy,
                                         scale=parl[:, G_MEM + k:G_MEM + k + 1]).then_inc(S["part_hi"], 1)
                    c.did("part_hi")

                def part_hi(out, in_):
                    c.own()
                    nc.scalar.activation(out, in_, ACT.Copy).then_inc(S["part_hi"], 1)
                    c.did("part_hi")

                h = H_KV
                for kind, e in ATT_STEPS:
                    if kind == "s":
                        continue
                    c.take("item_ready")
                    n = dict(K=A_KB, k=A_TK, V=A_VB, S=A_S, T=A_TP, O=A_PV)[kind][e]
                    s = slot_of(I_ATT + n)
                    if kind == "k":
                        part_hi(KTp[:, 0, 2 * e:2 * e + 2, :], bank(s, 0).rearrange("p (c m) -> p c m", c=2))
                    if kind == "V":
                        part_hi(Vp[0][:, :, e * 256:(e + 1) * 256], two(slot(s))[:, :, 0:256])
                    if kind == "S":
                        c.take("nmax_ready")
                        for t in range(4):
                            c.own()
                            last = "exp_done" if t == 3 else "a_step"
                            o = 4 + 16 * (e % 2)
                            nc.scalar.activation(prob[e % 2][:, t, :], slot(s)[:, t * 256:(t + 1) * 256], ACT.Exp,
                                                 bias=small[:, o + t:o + t + 1], scale=1.0 / 16,
                                                 accum_out=small[:, o + 4 + t:o + 5 + t]).then_inc(S[last], 1)
                            c.did(last)
                    if kind == "T":
                        part_hi(PT[:, 0, :, :], two(slot(s)))
                    if kind == "O":
                        part_hi(H[:, 0, 2 * e:2 * e + 2, 0:TP], two(slot(s)))
                    c.note("item_done")
                    if kind in "KV":
                        split(h + 4)
                        split(h + 5)
                        h += 2

                c.take("dec_zeroed", 2)

                def copy_keys(first, halves):
                    for j in halves:
                        c.take("k_turned")
                        if not (first and j < 2):
                            c.take("scores_done")
                        c.own()
                        nc.scalar.activation(k_dec[j % 2], slot(j % 2), ACT.Copy).then_inc(S["k_copied"], 1)
                        c.did("k_copied")

                def exps():
                    c.take("nmax_dec")
                    c.own()
                    nc.scalar.activation(p_dec, bank(2, 0, 0, 256), ACT.Exp, bias=small[:, 40:41], scale=1.0 / 16,
                                         accum_out=small[:, 41:42]).then_inc(S["dec_exp"], 1)
                    c.did("dec_exp")

                def output_hi(n):
                    c.take("o_turned")
                    for i in range(2):
                        c.own()
                        last = "o_hi" if i else "a_step"
                        nc.scalar.activation(dec_cols(H[:, 0], i, n),
                                             bank(3, 0, i * P, (i + 1) * P).rearrange("p (b h t) -> p b h t", b=2, h=4),
                                             ACT.Copy).then_inc(S[last], 1)
                        c.did(last)

                copy_keys(True, range(4))
                exps()
                with c.loop(0, 3, GROW_PAIR) as n:
                    copy_keys(False, range(4))
                    exps()
                    output_hi(n)
                output_hi(3)
                c.note("scores_done", 2)
                c.note("raw_full0", 8 * 16)
                c.note("raw_full1", 8 * 16)
                for m in range(KC):
                    update(m, H_WO + m, G_FFN[1])
                ffn(1)

            c.take("item_ready")
            c.note("item_done")
            c.take("recip_done")
            c.own()
            nc.scalar.activation(rstd[:, :], sqsum[:, :], ACT.Sqrt).then_inc(S["rstd_ready"], 1)
            for t in range(5):
                act.wait_ge(S["y_copied"], t + 1)
                dst = y_prompt[0, t * P:(t + 1) * P, :] if t < 4 else y_sample.rearrange("b t d -> (b t) d")
                act.dma_start(dst, Mf[:, t * D:(t + 1) * D]).then_inc(S["y_sent"], 16)
            act.wait_ge(S["y_sent"], 80)

        @block.vector
        def _(dve):
            c = Counts(dve, S, S["settled_dve"])
            TT = nc.vector.tensor_tensor

            def step(name="v_step"):
                c.own()
                c.did(name)
                return S[name]

            def split(h):
                c.take("w_hi")
                s = step("w_ready")
                TT(w_half(1, h), raw_half(h), w_half(0, h).bitcast(f32), ALU.subtract).then_inc(s, 1)

            def lo_part(m, gcol):
                c.take("xn_hi")
                s = step("xn_ready")
                nc.vector.scalar_tensor_tensor(out=X[:, 1, m, :], in0=xT[:, m, :],
                                               scalar=parl[:, gcol + m:gcol + m + 1],
                                               in1=X[:, 0, m, :].bitcast(f32), op0=ALU.mult,
                                               op1=ALU.subtract).then_inc(s, 1)
                c.take("x_sq")
                if m:
                    s = step("sq_added")
                    TT(sqsum[:, :], sqsum[:, :], sq[m % 2], ALU.add).then_inc(s, 1)

            def rms(n):
                s = step("item_done")
                nc.vector.tensor_scalar(two(sqsum[:, :]), tok(slot_of(n)), EPS, None, ALU.add).then_inc(s, 1)
                s = step("recip_done")
                nc.vector.reciprocal(sqsum[:, :], sqsum[:, :]).then_inc(s, 1)

            def scaled(out, n):
                s = step("item_done")
                TT(two(out), tok(slot_of(n)), two(rstd[:, :]), ALU.mult).then_inc(s, 1)

            def hidden_lo(chunk, v):
                c.take("hid_hi")
                s = step("hid_ready")
                TT(hidden(1, chunk), v, hidden(0, chunk).bitcast(f32), ALU.subtract).then_inc(s, 1)

            dve.wait_ge(S["consts"], 3 + PS)
            for h in range(4):
                split(h)
            dve.wait_ge(S["item_ready"], 1)
            s = step("item_done")
            nc.vector.tensor_copy(par[:, :], bank(0, 0, 0, 120)).then_inc(s, 1)
            s = step("par_ready")
            nc.vector.tensor_copy(parl[:, :], par[:, 0:64]).then_inc(s, 1)
            for t in range(5):
                dve.wait_ge(S["item_ready"], t + 2)
                s = step("item_done")
                nc.vector.tensor_copy(xT[:, :, t * P:(t + 1) * P],
                                      slot((t + 1) % 4).rearrange("p (k t) -> p k t", k=KC)).then_inc(s, 1)
            for m in range(KC):
                lo_part(m, 0)
            dve.wait_ge(S["mem_sq"], 2)
            s = step("v_step")
            nc.vector.tensor_scalar(small[:, 2:4], small[:, 0:2], 1.0 / D, EPS, ALU.mult, ALU.add).then_inc(s, 1)
            s = step("mem_ms")
            nc.vector.reciprocal(small[:, 2:4], small[:, 2:4]).then_inc(s, 1)
            dve.wait_ge(S["mem_rstd"], 1)
            for i in range(2):
                s = step("mem_scaled")
                nc.vector.tensor_scalar(Mf[:, (2 + i) * D:(3 + i) * D], Mf[:, (2 + i) * D:(3 + i) * D],
                                        small[:, 2 + i:3 + i], None, ALU.mult).then_inc(s, 1)
            for i in range(2):
                dve.wait_ge(S["item_ready"], 7 + i)
                s = step("item_done")
                nc.vector.tensor_copy(memT[:, :, i * P:(i + 1) * P],
                                      slot((6 + i) % 4).rearrange("p (k t) -> p k t", k=KC)).then_inc(s, 1)
            c.n["item_ready"] = N_PRO

            def first_item(n):
                c.take("item_ready", 2)
                rms(n)
                c.take("rstd_ready")

            def gate_up(q, n, h0, first):
                for e in range(2):
                    if first and e == 0:
                        first_item(n - 1)
                    else:
                        c.take("item_ready")
                    scaled(gate[e], n + e)
                    split(h0 + 4 + e)
                for e in range(2):
                    c.take("item_ready")
                    scaled(val[e], n + 2 + e)
                    c.take("gate_silu")
                    s = step("hid_f32")
                    TT(val[e], val[e], gate[e], ALU.mult).then_inc(s, 1)
                    hidden_lo(q(e), val[e])
                    split(h0 + 6 + e)

            def update(m, n, h, scale, gcol=None):
                c.take("item_ready")
                s = step("item_done")
                x = xT[:, m, :].rearrange("p a (b t) -> p (a b) t", b=2) if not isinstance(m, int) else two(xT[:, m, :])
                nc.vector.scalar_tensor_tensor(out=x, in0=tok(slot_of(n)), scalar=scale, in1=x, op0=ALU.mult,
                                               op1=ALU.add).then_inc(s, 1)
                if gcol is not None:
                    lo_part(m, gcol)
                split(h + 4)

            def ffn(w):
                h = (H_FFN0, H_FFN1)[w]
                for g, k in enumerate(GROUPS):
                    n, it = I_FFN[w] + FFN_IN[g], k // 2
                    if g == 0:
                        gate_up(lambda e: e, n, h, True)
                        n, it, h = n + 4, it - 1, h + 4
                    with c.loop(0, it, GROW_IN) as i:
                        gate_up(lambda e: i * 2 + (2 * (g == 0) + e), n, h, False)
                    h += 4 * it
                    n = I_FFN[w] + FFN_OUT[g]
                    if g < 2:
                        with c.loop(0, 2, GROW_OUT) as i:
                            for m in range(4):
                                update(ds(i * 4 + m, 1), n + m, h + m, 0.5)
                    else:
                        for m in range(KC):
                            update(m, n + m, h + m, 0.5, (G_MIX, G_NEXT)[w])
                    h += KC

            with c.loop(0, DEPTH, GROW_LAYER) as l:
                s = step("par_ready")
                nc.vector.tensor_copy(parl[:, :], par[:, ds(l * G_LAYER, 64)]).then_inc(s, 1)
                ffn(0)

                I = I_MIX
                c.take("pw_hi")
                s = step("pw_ready")
                TT(pw[:, 1, :, :], mrow[:, 0, :].rearrange("p (g f) -> p g f", g=4), pw[:, 0, :, :].bitcast(f32),
                   ALU.subtract).then_inc(s, 1)
                c.take("item_ready")
                s = step()
                nc.vector.tensor_copy(Mf[:, 5448:5928], bank(slot_of(I), 0, 0, 480)).then_inc(s, 1)
                s = step("item_done")
                nc.vector.tensor_copy(Mf[:, 5928:5992], bank(slot_of(I), 1, 0, 64)).then_inc(s, 1)

                def prefixed(ext, e, pfx, n):
                    s = step()
                    nc.vector.memset(ext[:, 0:n], 0.0).then_inc(s, 1)
                    s = step()
                    nc.vector.tensor_copy(samples(ext, n + TP, n + 16)[:, :, 0:n], pfx[:, e, :, :]).then_inc(s, 1)

                def pooled(e):
                    w = 2 << e
                    p, n = p_ext[e % 2], I + M_P[e]
                    prefixed(p, e, pfx_pool, PS)
                    r = rstd
                    s_ = slot_of(n)
                    s = step()
                    TT(p[:, PS:PS + HT], bank(s_, 0, 0, HT), r[:, 0:HT], ALU.mult).then_inc(s, 1)
                    s = step()
                    TT(p[:, PS + HT:PS + TP], bank(s_, 1, 0, TP - HT), r[:, HT:TP], ALU.mult).then_inc(s, 1)
                    s = step("item_done")
                    TT(samples(p, PS + TP, PS + 16)[:, :, PS:], samples(bank(s_, 1), TP - HT, 16),
                       samples(r, TP, 16), ALU.mult).then_inc(s, 1)
                    src, size = p, PX
                    for k in range(e + 1):
                        size -= 1 << k
                        s = step()
                        TT(sums[k % 2][:, 0:size], src[:, 0:size], src[:, (1 << k):(1 << k) + size],
                           ALU.add).then_inc(s, 1)
                        src = sums[k % 2]
                    v = val[e % 2]
                    o = PS - (w - 1)
                    s = step()
                    nc.vector.scalar_tensor_tensor(
                        out=samples(v, TP, 16), in0=samples(src, PS + TP, PS + 16)[:, :, o:o + 16],
                        scalar=1.0 / w, in1=samples(p, PS + TP, PS + 16)[:, :, PS:],
                        op0=ALU.mult, op1=ALU.subtract).then_inc(s, 1)
                    s = step()
                    nc.vector.scalar_tensor_tensor(out=v[:, w - 1:TP], in0=src[:, PS:PS + TP - w + 1],
                                                   scalar=1.0 / w, in1=p[:, PS + w - 1:PS + TP],
                                                   op0=ALU.mult, op1=ALU.subtract).then_inc(s, 1)
                    s = step()
                    TT(v[:, 0:w - 1], src[:, o:o + w - 1], invc[:, 0:w - 1], ALU.mult).then_inc(s, 1)
                    s = step("hid_f32")
                    TT(v[:, 0:w - 1], v[:, 0:w - 1], p[:, PS:PS + w - 1], ALU.subtract).then_inc(s, 1)
                    hidden_lo(4 + e, v)

                def state_rows(n, rows):
                    c.take("stage_free")
                    s_ = slot_of(n)
                    s = step()
                    r = 4 * (rows + 16)
                    nc.vector.tensor_copy(stage[0:r, 0:2, :], two(bank(s_, 0))[0:r]).then_inc(s, 1)
                    s = step("item_done")
                    nc.vector.tensor_copy(stage[0:16, 2, :], bank(s_, 1, 0, 256)[0:16, :]).then_inc(s, 1)

                def conv(e):
                    u, n = u_ext[e % 2], I + M_V[e]
                    scaled(val[e % 2], n)
                    prefixed(u, e, pfx_conv, 2)
                    s = step()
                    TT(u[:, 2:2 + TP], val[e % 2][:, 0:TP], gate[e % 2][:, 0:TP], ALU.mult).then_inc(s, 1)
                    s = step("v_step")
                    TT(samples(u, 2 + TP, 18)[:, :, 2:], samples(val[e % 2], TP, 16), samples(gate[e % 2], TP, 16),
                       ALU.mult).then_inc(s, 1)
                    t = p_ext[e % 2][:, 0:UX - 2]
                    for k in range(CW):
                        col = parl[:, G_CONV + 4 * k + e:G_CONV + 4 * k + e + 1]
                        s = step()
                        if k == 0:
                            nc.vector.tensor_scalar(t, u[:, 0:UX - 2], col, None, ALU.mult).then_inc(s, 1)
                        else:
                            nc.vector.scalar_tensor_tensor(out=t, in0=u[:, k:k + UX - 2], scalar=col, in1=t,
                                                           op0=ALU.mult, op1=ALU.add).then_inc(s, 1)

                def gated(e):
                    v, t = val[e % 2], p_ext[e % 2]
                    scaled(v, I + M_B[e])
                    s = step()
                    TT(v[:, 0:TP], v[:, 0:TP], t[:, 0:TP], ALU.mult).then_inc(s, 1)
                    s = step("hid_f32")
                    TT(samples(v, TP, 16), samples(v, TP, 16), samples(t, 2 + TP, 18)[:, :, 0:16],
                       ALU.mult).then_inc(s, 1)
                    hidden_lo(e, v)

                h = H_MIX
                for kind, e in MIX_STEPS:
                    if (kind, e) == ("P", 0):
                        first_item(I + 1)
                    elif (kind, e) == ("P", 2):
                        c.take("item_ready", 2)
                    elif (kind, e) != ("p", 0):
                        c.take("item_ready")
                    if kind == "P":
                        pooled(e)
                    elif kind == "p":
                        state_rows(I + M_SP[e], PS)
                    elif kind == "C":
                        scaled(gate[e % 2], I + M_C[e])
                    elif kind == "V":
                        conv(e)
                    elif kind == "B":
                        gated(e)
                    elif kind == "c":
                        state_rows(I + M_SC[e], 2)
                    elif kind == "W":
                        c.take("part_hi")
                        s = step("item_done")
                        nc.vector.scalar_tensor_tensor(out=two(H[:, 1, 4 + e, :]), in0=tok(slot_of(I + M_PW[e])),
                                                       scalar=parl[:, G_PSCALE + e:G_PSCALE + e + 1],
                                                       in1=two(Hf[:, 0, 4 + e, :]), op0=ALU.mult,
                                                       op1=ALU.subtract).then_inc(s, 1)
                    if kind in "PCVB":
                        split(h + 4)
                        h += 1
                for m in range(KC):
                    update(m, I + M_OUT + m, h + m, 1.0, G_ATT)

                def place_queries(n):
                    for i in range(2):
                        s = step("q_placed" if i else "v_step")
                        TT(diag(qblk, i).rearrange("p (b h) t -> p b h t", b=2), dec_cols(Hf[:, 0], i, n),
                           dec_cols(Hf[:, 1], i, n), ALU.add).then_inc(s, 1)

                I = I_ATT
                for m in range(KC):
                    if m == 0:
                        first_item(I)
                    else:
                        c.take("item_ready")
                    scaled(val[m % 2], I + A_Q + m)
                    hidden_lo(m, val[m % 2])
                    split(H_Q + 4 + m)
                for k in range(KC):
                    c.take("part_hi")
                    s = step("memx_ready")
                    nc.vector.scalar_tensor_tensor(out=memx[:, 1, k, :], in0=memT[:, k, :],
                                                   scalar=parl[:, G_MEM + k:G_MEM + k + 1],
                                                   in1=memx[:, 0, k, :].bitcast(f32), op0=ALU.mult,
                                                   op1=ALU.subtract).then_inc(s, 1)
                h = H_KV
                for kind, e in ATT_STEPS:
                    if kind == "s":
                        o = 4 + 16 * (e % 2)
                        for t in range(4):
                            s = step("prob_ready" if t == 3 else "v_step")
                            nc.vector.tensor_scalar(prob[e % 2][:, t, :], prob[e % 2][:, t, :],
                                                    small[:, o + 8 + t:o + 9 + t], None, ALU.mult).then_inc(s, 1)
                        continue
                    if (kind, e) == ("T", 3):
                        c.take("dec_zeroed")
                        place_queries(0)
                    c.take("item_ready")
                    s_ = slot_of(I + dict(K=A_KB, k=A_TK, V=A_VB, S=A_S, T=A_TP, O=A_PV)[kind][e])
                    if kind == "K":
                        if e >= 2:
                            c.take("k_sent")
                        s = step("item_done")
                        nc.vector.tensor_copy(kv_st[e % 2], two(slot(s_))[:, :, 0:256]).then_inc(s, 1)
                    elif kind == "k":
                        c.take("part_hi")
                        s = step("item_done")
                        TT(KTp[:, 1, 2 * e:2 * e + 2, :], bank(s_, 0).rearrange("p (c m) -> p c m", c=2),
                           KTp[:, 0, 2 * e:2 * e + 2, :].bitcast(f32), ALU.subtract).then_inc(s, 1)
                    elif kind == "V":
                        if e >= 2:
                            c.take("k_sent", 3 if e == 2 else 1)
                        c.take("part_hi")
                        s = step()
                        nc.vector.tensor_copy(kv_st[2 + e % 2], two(slot(s_))[:, :, 0:256]).then_inc(s, 1)
                        s = step("item_done")
                        TT(Vp[1][:, :, e * 256:(e + 1) * 256], two(slot(s_))[:, :, 0:256],
                           Vp[0][:, :, e * 256:(e + 1) * 256].bitcast(f32), ALU.subtract).then_inc(s, 1)
                    elif kind == "S":
                        o = 4 + 16 * (e % 2)
                        s = step()
                        nc.vector.tensor_reduce(small[:, o + 12:o + 16], slot(s_).rearrange("p (t m) -> p t m", t=4),
                                                axis=AX.X, op=ALU.max).then_inc(s, 1)
                        s = step("nmax_ready")
                        nc.vector.tensor_scalar(small[:, o:o + 4], small[:, o + 12:o + 16], -1.0 / 16, None,
                                                ALU.mult).then_inc(s, 1)
                        c.take("exp_done")
                        s = step("item_done")
                        nc.vector.reciprocal(small[:, o + 8:o + 12], small[:, o + 4:o + 8]).then_inc(s, 1)
                    elif kind == "T":
                        c.take("part_hi")
                        s = step("item_done")
                        TT(PT[:, 1, :, :], two(slot(s_)), PT[:, 0, :, :].bitcast(f32), ALU.subtract).then_inc(s, 1)
                    elif kind == "O":
                        c.take("part_hi")
                        s = step("item_done")
                        TT(H[:, 1, 2 * e:2 * e + 2, 0:TP], two(slot(s_)), Hf[:, 0, 2 * e:2 * e + 2, 0:TP],
                           ALU.subtract).then_inc(s, 1)
                    if kind in "KV":
                        split(h + 4)
                        split(h + 5)
                        h += 2
                c.note("k_sent", 2)

                c.take("dec_zeroed")

                def maxima():
                    c.take("scores_done", 4)
                    s = step()
                    nc.vector.tensor_reduce(small[:, 43:44], bank(2, 0, 0, 256), axis=AX.X, op=ALU.max).then_inc(s, 1)
                    s = step("nmax_dec")
                    nc.vector.tensor_scalar(small[:, 40:41], small[:, 43:44], -1.0 / 16, None, ALU.mult)\
                        .then_inc(s, 1)

                def probabilities():
                    c.take("dec_exp")
                    s = step()
                    nc.vector.reciprocal(small[:, 42:43], small[:, 41:42]).then_inc(s, 1)
                    s = step("p_scaled")
                    nc.vector.tensor_scalar(p_dec, p_dec, small[:, 42:43], None, ALU.mult).then_inc(s, 1)

                def place_probabilities():
                    c.take("p_turned")
                    for i in range(2):
                        s = step("p_placed" if i else "v_step")
                        nc.vector.tensor_copy(diag(pblk, i), bank(2, 1, i * P, (i + 1) * P)
                                              .rearrange("p (e t) -> p e t", e=8)).then_inc(s, 1)

                def output_lo(n):
                    c.take("o_turned")
                    c.take("o_hi")
                    for i in range(2):
                        s = step("o_placed" if i else "v_step")
                        TT(dec_cols(H[:, 1], i, n), bank(3, 0, i * P, (i + 1) * P)
                           .rearrange("p (b h t) -> p b h t", b=2, h=4), dec_cols(Hf[:, 0], i, n),
                           ALU.subtract).then_inc(s, 1)

                def copy_output():
                    c.take("raw_used", 2)
                    s = step("o_copied")
                    nc.vector.tensor_copy(o_dec, bank(3, 1, 0, 256)).then_inc(s, 1)

                maxima()
                with c.loop(0, 3, GROW_PAIR) as n:
                    place_queries(n + 1)
                    probabilities()
                    place_probabilities()
                    maxima()
                    copy_output()
                    output_lo(n)
                probabilities()
                place_probabilities()
                copy_output()
                output_lo(3)
                for m in range(KC):
                    update(m, I + A_WO + m, H_WO + m, 1.0, G_FFN[1])
                ffn(1)

            c.take("item_ready")
            s = step("item_done")
            nc.vector.tensor_scalar(two(sqsum[:, :]), tok(slot_of(0)), EPS, None, ALU.add).then_inc(s, 1)
            s = step("recip_done")
            nc.vector.reciprocal(sqsum[:, :], sqsum[:, :]).then_inc(s, 1)
            c.take("rstd_ready")
            for m in range(KC):
                s = step("y_made")
                nc.vector.scalar_tensor_tensor(out=xT[:, m, :], in0=xT[:, m, :],
                                               scalar=parl[:, G_NEXT + m:G_NEXT + m + 1], in1=rstd[:, :],
                                               op0=ALU.mult, op1=ALU.mult).then_inc(s, 1)
            for t in range(5):
                c.take("item_ready")
                c.note("item_done")
                s = step("y_copied")
                nc.vector.tensor_copy(Mf[:, t * D:(t + 1) * D], slot(slot_of(t + 1))).then_inc(s, 1)

        @block.tensor
        def _(pe):
            c = Counts(pe, S, S["settled_pe"])
            mm = nc.tensor.matmul

            def three_passes(outs, k, K, lhs, rhs):
                last = None
                for n, (a, b) in enumerate(((0, 0), (0, 1), (1, 0))):
                    for o, out in enumerate(outs):
                        last = mm(out, lhs(a, o), rhs(b, o), start=(k == 0 and n == 0), stop=(k == K - 1 and n == 2))
                return last

            def token_item(n, h, moving, K=KC, ready=None):
                c.take("item_done")
                c.take("w_ready")
                s = slot_of(n)
                for k in range(K):
                    if ready:
                        ready(k)
                    last = three_passes([bank(s, b, 0, HT) for b in range(2)], k, K,
                                        lambda a, o: w_half(a, h)[:, k, :],
                                        lambda a, o: moving[:, a, k, o * HT:(o + 1) * HT])
                last.then_inc(S["item_ready"], 1)
                c.note("item_ready")

            def norm_item(n):
                c.take("sq_added", 7)
                norm_sum(slot_of(n))

            def norm_sum(s):
                for b in range(2):
                    last = mm(bank(s, b, 0, HT), onesd[:, :], sqsum[:, b * HT:(b + 1) * HT], start=True, stop=True)
                last.then_inc(S["item_ready"], 1)
                c.note("item_ready")

            def turn(out, in_, k=P):
                return nc.tensor.transpose(out, in_, ident[0:k, 0:k])

            def chunk_ready(name):
                at = {}

                def ready(k):
                    at.setdefault(k, c.value(name, k + 1))
                    pe.wait_ge(S[name], at[k])
                return ready

            pe.wait_ge(S["consts"], 3 + PS)
            pe.wait_ge(S["rows_loaded"], 16 * PARAM_LOADS)
            turn(bank(0, 0, 0, 120), mrow[0:120, 0, 0:P], 120).then_inc(S["item_ready"], 1)
            pe.wait_ge(S["x_loaded"], 80)
            for t in range(5):
                if t == 3:
                    pe.wait_ge(S["item_done"], 1)
                if t == 4:
                    pe.wait_ge(S["item_done"], 2)
                for k in range(KC):
                    last = turn(slot((t + 1) % 4)[:, k * P:(k + 1) * P], Mf[:, t * D + k * P:t * D + (k + 1) * P])
                last.then_inc(S["item_ready"], 1)
            pe.wait_ge(S["mem_scaled"], 2)
            pe.wait_ge(S["item_done"], 4)
            for i in range(2):
                for k in range(KC):
                    last = turn(slot((6 + i) % 4)[:, k * P:(k + 1) * P],
                                Mf[:, (2 + i) * D + k * P:(2 + i) * D + (k + 1) * P])
                last.then_inc(S["item_ready"], 1)
            c.note("item_ready", N_PRO)
            c.note("item_done", N_PRO - 4)

            def stage_first(n, h):
                c.take("item_done", 1)
                xn = chunk_ready("xn_ready")
                token_item(n + 1, h, X[:, :, :, :], ready=xn)
                c.note("xn_ready", KC)
                norm_item(n)

            def four(n, h, moving, K=KC, ready=None):
                for m in range(4):
                    token_item(n + m, h + m, moving, K, ready if m == 0 else None)

            def ffn(w):
                h = (H_FFN0, H_FFN1)[w]
                for g, k in enumerate(GROUPS):
                    n, it = I_FFN[w] + FFN_IN[g], k // 2
                    if g == 0:
                        stage_first(n - 1, h)
                        for m in range(1, 4):
                            token_item(n + m, h + m, X)
                        n, it, h = n + 4, it - 1, h + 4
                    with c.loop(0, it, GROW_OUT) as i:
                        four(n, h, X)
                    h += 4 * it
                    n = I_FFN[w] + FFN_OUT[g]
                    ready = chunk_ready("hid_ready")
                    with c.loop(0, 2, GROW_OUT) as i:
                        four(n, h, H, k, ready)
                    c.note("hid_ready", k)
                    h += KC

            with c.loop(0, DEPTH, GROW_LAYER) as l:
                ffn(0)

                I, h = I_MIX, H_MIX
                c.take("misc_loaded", 48)
                c.take("item_done")
                s = slot_of(I)
                for g in range(4):
                    turn(bank(s, 0, g * 120, (g + 1) * 120), mrow[0:120, 1, g * P:(g + 1) * P], 120)
                for g in range(4):
                    last = turn(bank(s, 1, g * 16, (g + 1) * 16), mrow[0:16, 2, g * P:(g + 1) * P], 16)
                last.then_inc(S["item_ready"], 1)
                c.note("item_ready")

                def state_item(n, ext, n0, after):
                    c.take("item_done")
                    pe.wait_ge(S[after[0]], after[1])
                    s = slot_of(n)
                    r = 4 * (n0 + 16)
                    for j in range(2):
                        for i in range(2):
                            turn(bank(s, 0, i * 256 + j * P, i * 256 + (j + 1) * P)[0:r],
                                 ext[j][:, n0 + TP + i * r:n0 + TP + (i + 1) * r])
                        last = turn(bank(s, 1, j * P, (j + 1) * P)[0:16, :], ext[j][:, n0 + TP - 16:n0 + TP])
                    last.then_inc(S["item_ready"], 1)
                    c.note("item_ready")

                for kind, e in MIX_STEPS:
                    if (kind, e) == ("P", 0):
                        stage_first(I + 1, h)
                        h += 1
                    elif kind in "PCVB":
                        token_item(I + dict(P=M_P, C=M_C, V=M_V, B=M_B)[kind][e], h, X)
                        h += 1
                    elif kind == "p":
                        state_item(I + M_SP[e], p_ext, PS, ("item_done", done_value(l, I + M_P[2 * e + 1])))
                    elif kind == "c":
                        state_item(I + M_SC[e], u_ext, 2, ("item_done", done_value(l, I + M_B[2 * e])))
                    elif kind == "W":
                        if e == 0:
                            c.take("pw_ready")
                        c.take("item_done")
                        c.take("hid_ready")
                        s = slot_of(I + M_PW[e])
                        three_passes([bank(s, b, 0, HT) for b in range(2)], 0, 1, lambda a, o: pw[:, a, e, :],
                                     lambda a, o: H[:, a, 4 + e, o * HT:(o + 1) * HT]).then_inc(S["item_ready"], 1)
                        c.note("item_ready")
                ya = chunk_ready("hid_ready")

                def y_ready(k):
                    if k < 4:
                        ya(k)
                    elif k == 4:
                        pe.wait_ge(S["item_done"], done_value(l, I + M_PW[3]))
                four(I + M_OUT, h, H, KC, y_ready)
                c.note("hid_ready", 4)
                four(I + M_OUT + 4, h + 4, H)

                I = I_ATT
                stage_first(I, H_Q)
                for m in range(1, KC):
                    token_item(I + A_Q + m, H_Q + m, X)
                mem_chunk = chunk_ready("memx_ready")

                def kv_item(n, h, ready=None):
                    c.take("item_done")
                    c.take("w_ready", 2)
                    s = slot_of(n)
                    for k in range(KC):
                        if ready:
                            ready(k)
                        last = three_passes([bank(s, b, 0, 256) for b in range(2)], k, KC,
                                            lambda a, o: memx[:, a, k, o * P:(o + 1) * P],
                                            lambda a, o: W[:, a, h % 4:h % 4 + 2, :]
                                            .rearrange("p f (k n) -> p f k n", n=P)[:, :, k, :])
                    last.then_inc(S["item_ready"], 1)
                    c.note("item_ready")

                h = H_KV
                for kind, e in ATT_STEPS:
                    if kind == "s":
                        continue
                    if kind in "KV":
                        kv_item(I + (A_KB if kind == "K" else A_VB)[e], h, mem_chunk if (kind, e) == ("K", 0) else None)
                        if (kind, e) == ("K", 0):
                            c.note("memx_ready", KC)
                        h += 2
                        continue
                    c.take("item_done")
                    s = slot_of(I + dict(k=A_TK, S=A_S, T=A_TP, O=A_PV)[kind][e])
                    if kind == "k":
                        pe.wait_ge(S["item_done"], done_value(l, I + A_KB[e]))
                        for i in range(2):
                            for m in range(2):
                                last = turn(bank(s, 0, i * 256 + m * P, i * 256 + (m + 1) * P),
                                            kv_st[e % 2][:, m, i * P:(i + 1) * P])
                    elif kind == "S":
                        pe.wait_ge(S["item_done"], done_value(l, I + A_TK[e]))
                        if e == 0:
                            c.take("hid_ready", KC)
                        for t in range(4):
                            for i in range(2):
                                last = three_passes([slot(s)[:, t * 256:(t + 1) * 256]], i, 2,
                                                    lambda a, o: H[:, a, 2 * e + i, t * P:(t + 1) * P],
                                                    lambda a, o: KTp[:, a, 2 * e + i, :])
                    elif kind == "T":
                        c.take("prob_ready")
                        for t in range(4):
                            for m in range(2):
                                last = turn(bank(s, m, t * P, (t + 1) * P), prob[e % 2][:, t, m * P:(m + 1) * P])
                    elif kind == "O":
                        pe.wait_ge(S["item_done"], done_value(l, I + A_TP[e]))
                        for i in range(2):
                            for m in range(2):
                                last = three_passes([bank(s, i)], m, 2,
                                                    lambda a, o: Vp[a][:, m, e * 256 + i * P:e * 256 + (i + 1) * P],
                                                    lambda a, o: PT[:, a, m, :])
                    last.then_inc(S["item_ready"], 1)
                    c.note("item_ready")

                pe.wait_ge(S["item_done"], done_value(l, I + A_PV[3]))

                def turn_keys(j):
                    if j % 2 == 0:
                        c.take(f"raw_full{j // 2}", 16)
                    for k in range(4):
                        for m in range(2):
                            f = (j % 2) * 4 + k
                            last = turn(slot(j % 2)[:, k * 256 + m * P:k * 256 + (m + 1) * P],
                                        raw[:, j // 2, m * D + f * P:m * D + (f + 1) * P])
                    last.then_inc(S["k_turned"], 1)
                    c.note("k_turned")

                def score(j):
                    c.take("k_copied")
                    for k in range(4):
                        f = (j % 2) * 4 + k
                        e = (j // 2) * 4 + f // 2
                        blk = (f % 2) * 1024 + e * P
                        last = mm(bank(2, 0, 0, 256), qblk[:, blk:blk + P], k_dec[j % 2][:, k * 256:(k + 1) * 256],
                                  start=(j == 0 and k == 0), stop=(j == 3 and k == 3))
                    last.then_inc(S["scores_done"], 1)
                    c.note("scores_done")

                def turn_probabilities():
                    c.take("p_scaled")
                    for m in range(2):
                        last = turn(bank(2, 1, m * P, (m + 1) * P), p_dec[:, m * P:(m + 1) * P])
                    last.then_inc(S["p_turned"], 1)
                    c.note("p_turned")

                def output():
                    c.take("p_placed")
                    for b in range(2):
                        c.take(f"raw_full{b}", 16)
                        for hd in range(NH):
                            e = b * NH + hd
                            for m in range(2):
                                last = mm(bank(3, 1, 0, 256), pblk[:, m * 1024 + e * P:m * 1024 + (e + 1) * P],
                                          raw[:, b, m * D + hd * 256:m * D + (hd + 1) * 256],
                                          start=(e == 0 and m == 0), stop=(e == 7 and m == 1))
                        last.then_inc(S["raw_used"], 1)
                        c.note("raw_used")

                def turn_output():
                    c.take("o_copied")
                    for i in range(2):
                        last = turn(bank(3, 0, i * P, (i + 1) * P), o_dec[:, i * P:(i + 1) * P])
                    last.then_inc(S["o_turned"], 1)
                    c.note("o_turned")

                c.n["raw_full0"] = c.n["raw_full1"] = 30 * 16
                turn_keys(0)
                turn_keys(1)
                c.take("q_placed")
                score(0)
                turn_keys(2)
                score(1)
                turn_keys(3)
                score(2)
                score(3)
                with c.loop(0, 3, GROW_PAIR) as n:
                    turn_keys(0)
                    turn_keys(1)
                    c.take("q_placed")
                    c.take("dec_exp")
                    score(0)
                    turn_keys(2)
                    score(1)
                    turn_keys(3)
                    turn_probabilities()
                    score(2)
                    score(3)
                    output()
                    turn_output()
                turn_probabilities()
                output()
                turn_output()
                c.note("dec_exp")
                c.take("o_placed", 4)
                c.n["raw_full0"] = c.n["raw_full1"] = 56 * 16
                four(I + A_WO, H_WO, H)
                four(I + A_WO + 4, H_WO + 4, H)
                ffn(1)

            c.take("item_done")
            c.take("sq_added", 7)
            norm_sum(slot_of(0))
            pe.wait_ge(S["y_made"], KC)
            for t in range(5):
                if t == 3:
                    c.take("item_done", 4)
                if t == 4:
                    pe.wait_ge(S["y_copied"], 1)
                for k in range(KC):
                    last = turn(slot(slot_of(t + 1))[:, k * P:(k + 1) * P], xT[:, k, t * P:(t + 1) * P])
                last.then_inc(S["item_ready"], 1)
                c.note("item_ready")


def parameter_rows(ffn_norm, mix_norm, xattn_norm, mem_norm, pool_scale, conv_w, final_norm):
    def rows(v):
        return v.rearrange("(m p) -> m p", p=P)

    for l in range(DEPTH):
        r = l * G_LAYER
        yield r + G_FFN[0], rows(ffn_norm[l, 0])
        yield r + G_FFN[1], rows(ffn_norm[l, 1])
        yield r + G_MIX, rows(mix_norm[l])
        yield r + G_ATT, rows(xattn_norm[l])
        yield r + G_MEM, rows(mem_norm[l])
        yield r + G_PSCALE, rows(pool_scale[l])
        yield r + G_CONV, conv_w[l].rearrange("k (j p) -> (k j) p", p=P)
    yield DEPTH * G_LAYER, rows(final_norm)


INPUTS = ["x_prompt", "x_sample", "mem_prompt", "cache_mem_k", "cache_mem_v", "state_conv", "state_pool", "ffn_norm",
          "ffn_w_in", "ffn_w_out", "mix_norm", "mix_w_in", "conv_w", "pool_w", "pool_scale", "mix_w_out",
          "xattn_norm", "mem_norm", "xattn_wq", "xattn_wkv", "xattn_wo", "final_norm"]
OUTPUTS = [(1, TP, D), (NB, 16, D), (DEPTH, 1, NMEM, NH, 256), (DEPTH, 1, NMEM, NH, 256), (DEPTH, 1, 2, DC),
           (DEPTH, 1, PS, DC), (DEPTH, NB, 2, DC), (DEPTH, NB, PS, DC)]


def kernel(**inputs):
    import numpy as np
    import concourse.bacc as bacc
    from concourse.bass_utils import run_bass_kernel_spmd

    nc = bacc.Bacc("TRN2", target_bir_lowering=False, num_devices=1)
    arrays, args = {}, []
    for name in INPUTS:
        a = np.ascontiguousarray(inputs[name])
        arrays[f"in_{name}"] = a
        args.append(nc.dram_tensor(f"in_{name}", a.shape, mybir.dt.from_np(a.dtype), kind="ExternalInput").ap())
    for i, shape in enumerate(OUTPUTS):
        args.append(nc.dram_tensor(f"out_{i}", shape, mybir.dt.float32, kind="ExternalOutput").ap())
    program(nc, *args)
    r = run_bass_kernel_spmd(nc, [arrays], core_ids=[0])
    return tuple(r.results[0][f"out_{i}"] for i in range(len(OUTPUTS)))
```

```python
import concourse.bass as bass
from concourse import mybir
from contextlib import ExitStack

D = 1024
P = 128
DEPTH = 2
TP, NB, TD = 512, 8, 16
T = TP + NB * TD
HT = T // 2
DC = 512
DFF = 2816
NMEM = 256
NH = 4
CW = 3
PS = 15
EPS = 1e-6
KC = D // P
GROUPS = (8, 8, 6)
GSTART = (0, 8, 16)

R_FFN, R_FINAL, R_GAINS, R_PSCALE, R_CONV = 0, 32, 40, 88, 96
N_PAR = 120
G_FFN, G_NEXT, G_MIX, G_ATT, G_MEM, G_PSCALE, G_CONV = (0, 8), 16, 24, 32, 40, 48, 52

N_FFN = 69
FFN_IN = (1, 25, 49)
FFN_OUT = (17, 41, 61)
M_P, M_SP = (2, 3, 6, 8), (7, 10)
M_C, M_V, M_B = (4, 5, 19, 20), (9, 11, 21, 22), (14, 16, 23, 25)
M_PW, M_SC = (12, 13, 17, 18), (15, 24)
M_OUT = 26
N_MIX = 34
A_Q = 1
A_KB, A_TK = (9, 10, 12, 14), (11, 13, 15, 17)
A_VB, A_S, A_TP, A_PV = (16, 19, 21, 22), (18, 20, 25, 26), (23, 24, 29, 30), (27, 28, 31, 32)
A_WO = 33
N_ATT = 41
I_FFN = (0, N_FFN + N_MIX + N_ATT)
I_MIX, I_ATT = N_FFN, N_FFN + N_MIX
N_LAYER = 2 * N_FFN + N_MIX + N_ATT
SHIFT = -N_LAYER % 4
N_PRO = 8
MIX_STEPS = [("P", 0), ("P", 1), ("C", 0), ("C", 1), ("P", 2), ("p", 0), ("P", 3), ("V", 0), ("p", 1), ("V", 1),
             ("W", 0), ("W", 1), ("B", 0), ("c", 0), ("B", 1), ("W", 2), ("W", 3), ("C", 2), ("C", 3), ("V", 2),
             ("V", 3), ("B", 2), ("c", 1), ("B", 3)]
ATT_STEPS = [("K", 0), ("K", 1), ("k", 0), ("K", 2), ("k", 1), ("K", 3), ("k", 2), ("V", 0), ("k", 3), ("S", 0),
             ("V", 1), ("S", 1), ("V", 2), ("V", 3), ("T", 0), ("T", 1), ("S", 2),
             ("S", 3), ("O", 0), ("O", 1), ("T", 2), ("T", 3), ("O", 2), ("O", 3)]
LATE = {("T", 2): ("V", 2), ("T", 3): ("V", 3)}
HID_Q = 38

KEY_SLOTS, SCORE_SLOT, OUT_SLOT = (1, 0), 3, 2

H_FFN0, H_MIX, H_Q, H_KV, H_WO, H_FFN1 = 0, 68, 92, 100, 116, 124
GROW_A_STEP, GROW_V_STEP = 20, 116

GROW_IN = dict(item_ready=4, item_done=4, w_hi=4, w_ready=4, raw_full0=16, raw_full1=16, gate_silu=2,
               hid_f32=2, hid_hi=2, hid_ready=2)
GROW_OUT = dict(item_ready=4, item_done=4, w_hi=4, w_ready=4, raw_full0=16, raw_full1=16)
GROW_BLOCKS = dict(w_ready=4, raw_full0=16, raw_full1=16)
GROW_PAIR = dict(k_turned=4, k_copied=4, scores_done=4, q_placed=1, nmax_dec=1, dec_exp=1, p_scaled=1, p_turned=1, p_placed=1,
                 raw_used=2, o_copied=1, o_turned=1, o_hi=1, o_placed=1, raw_full0=32, raw_full1=32, a_step=1,
                 v_step=5)
GROW_LAYER = dict(item_ready=N_LAYER, item_done=N_LAYER, w_hi=192, w_ready=192, raw_full0=56 * 16,
                  raw_full1=56 * 16, gate_silu=44, hid_f32=52, hid_hi=60, hid_ready=60, xn_hi=32, x_sq=32,
                  xn_ready=32, sq_added=28, recip_done=4, rstd_ready=4, par_ready=1, misc_loaded=48, pw_hi=1,
                  pw_ready=1, part_hi=28, memx_ready=8, exp_done=4, prob_ready=4, stage_free=4, k_sent=8, dec_zeroed=2,
                  k_turned=16, k_copied=16, scores_done=16, q_placed=4, dec_exp=4, p_scaled=4, p_turned=4,
                  p_placed=4, raw_used=8, o_copied=4, o_turned=4, o_hi=4, o_placed=4, a_step=GROW_A_STEP,
                  v_step=GROW_V_STEP, stage_sent=64 * (NB + 1), kv_sent=128, nmax_ready=4, nmax_dec=4)


PARAM_LOADS = 7


class Counts:

    def __init__(self, eng, sems, settled, settles=False):
        self.settled = settled
        self.eng, self.sems, self.n, self.turns, self.last, self.settles = eng, sems, {}, [], None, settles

    def value(self, name, more=0):
        v = self.n.get(name, 0) + more
        for i, grow in self.turns:
            if grow.get(name, 0):
                v = i * grow[name] + v
        return v

    def take(self, name, n=1):
        self.n[name] = self.n.get(name, 0) + n
        self.eng.wait_ge(self.sems[name], self.value(name))
        if self.settles:
            self.settle()

    def settle(self):
        self.eng.sem_inc(self.settled, 1)

    def note(self, name, n=1):
        self.n[name] = self.n.get(name, 0) + n

    def did(self, name):
        self.note(name)
        self.last = name

    def own(self):
        if self.last:
            self.eng.wait_ge(self.sems[self.last], self.value(self.last))

    def loop(self, lo, hi, grow):
        return Turns(self, lo, hi, grow)


class Turns:

    def __init__(self, counts, lo, hi, grow):
        self.c, self.lo, self.hi, self.grow = counts, lo, hi, grow

    def __enter__(self):
        self.c.own()
        self.c.last = None
        self.c.settle()
        self.f = self.c.eng.Fori(self.lo, self.hi)
        i = self.f.__enter__()
        self.start = dict(self.c.n)
        if self.lo:
            for name, n in self.grow.items():
                self.c.n[name] = self.c.n.get(name, 0) - self.lo * n
        self.inside = dict(self.c.n)
        self.c.turns.append((i, self.grow))
        return i

    def __exit__(self, *error):
        if error[0]:
            return False
        self.c.own()
        self.c.last = None
        grown = {k: v - self.inside.get(k, 0) for k, v in self.c.n.items() if v != self.inside.get(k, 0)}
        wrong = {k: v for k, v in grown.items() if v != self.grow.get(k, 0)}
        assert not wrong, f"{self.c.eng.engine}: grown {wrong}"
        self.c.turns.pop()
        self.f.__exit__(None, None, None)
        self.c.n = {**self.start, **{k: self.start.get(k, 0) + (self.hi - self.lo) * v for k, v in grown.items()}}


def program(nc, x_prompt, x_sample, mem_prompt, cache_k, cache_v, state_conv, state_pool, ffn_norm,
            ffn_w_in, ffn_w_out, mix_norm, mix_w_in, conv_w, pool_w, pool_scale, mix_w_out,
            xattn_norm, mem_norm, wq, wkv, wo, final_norm,
            y_prompt, y_sample, mem_k_out, mem_v_out, conv_p_out, pool_p_out, conv_s_out, pool_s_out):
    f32, f32r = mybir.dt.float32, mybir.dt.float32r
    ALU, ACT, AX = mybir.AluOpType, mybir.ActivationFunctionType, mybir.AxisListType
    ds = bass.ds

    ctx = ExitStack()
    with ctx:
        def sb(name, shape, dt=f32):
            return ctx.enter_context(nc.sbuf_tensor(name, shape, dt))

        xT = sb("xT", [P, KC, T])
        X = sb("X", [P, 2, KC, T], f32r)
        Xflat = X[:, :, :, :].rearrange("p a k t -> p (a k t)")
        H = sb("H", [P, 2, KC, T], f32r)
        Hf = H[:, :, :, :].bitcast(f32)
        raw = sb("raw", [P, 2, 2048])
        W = sb("W", [P, 2, 4, 1024], f32r)
        Mr = sb("Mr", [P, 2048], f32r)
        Mf = sb("Mf", [P, 7040])
        memT = sb("memT", [P, KC, NMEM])
        sqsum = sb("sqsum", [P, T])
        rstd = sb("rstd", [P, T])
        mrow = sb("mrow", [P, 3, DC])
        stage = sb("stage", [P, 3, 256])
        ident = sb("ident", [P, P])
        onesd = sb("onesd", [P, P])
        par = sb("par", [P, 120])
        parl = sb("parl", [P, 64])
        invc = sb("invc", [P, 16])
        small = sb("small", [P, 48])
        mem_rows = memT[:, :, :].rearrange("p k m -> p (k m)").rearrange("p (c d) -> p c d", c=2)
        gain_row = Mf[:, 5 * D:6 * D]
        psum = ctx.enter_context(nc.psum_tensor("psum", [P, 4096], f32))

        tmp = [Mf[:, i * T:(i + 1) * T] for i in range(4)]
        gate, val, sq = tmp[0:2], tmp[2:4], tmp[0:2]
        PX = PS + TP + NB * (PS + 16)
        UX = 2 + TP + NB * 18
        p_ext = [Mf[:, 2580 + i * 776:2580 + i * 776 + PX] for i in range(2)]
        u_ext = [Mf[:, 4132 + i * UX:4132 + (i + 1) * UX] for i in range(2)]
        sums = [Mf[:, 5992:5992 + PX], Mf[:, 4132:4132 + PX]]
        taps = [sums[0], p_ext[1]]
        pfx_pool = Mf[:, 5448:5928].rearrange("p (g b t) -> p g b t", g=4, t=PS)
        pfx_conv = Mf[:, 5928:5992].rearrange("p (g b t) -> p g b t", g=4, t=2)
        kv_st = [Mf[:, 2560 + i * 512:2560 + (i + 1) * 512].rearrange("p (c f) -> p c f", c=2) for i in range(4)]
        prob = [Mf[:, 4608 + i * 1024:4608 + (i + 1) * 1024].rearrange("p (t m) -> p t m", t=4) for i in range(2)]
        qblk, pblk = Mf[:, 0:2176], Mf[:, 2176:4352]
        k_dec = [Mf[:, 4352 + i * 1024:4352 + (i + 1) * 1024] for i in range(2)]
        p_dec, o_dec = Mf[:, 6400:6656], Mf[:, 6656:6912]
        KTp = Xflat[:, 0:4096].rearrange("p (a k m) -> p a k m", a=2, k=KC)
        memx = Xflat[:, 4096:8192].rearrange("p (a k m) -> p a k m", a=2, k=KC)
        PT = [Xflat[:, 4096 + i * 2048:6144 + i * 2048].rearrange("p (a c t) -> p a c t", a=2, c=2) for i in range(2)]
        Vp = [Xflat[:, 8192:10240].rearrange("p (c f) -> p c f", c=2), Mr[:, :].rearrange("p (c f) -> p c f", c=2)]
        pw = Mr[:, 0:1024].rearrange("p (a g f) -> p a g f", a=2, g=4)

        names = """x_loaded0 x_loaded1 x_loaded2 x_loaded3 x_loaded4 x_copied counts_made mem_loaded rows_loaded misc_loaded consts raw_full0 raw_full1 w_hi w_ready item_ready
            item_done mem_sq mem_ms mem_rstd xn_hi x_sq xn_ready sq_added recip_done rstd_ready gate_silu hid_f32
            hid_hi hid_ready par_ready pw_hi pw_ready part_hi memx_ready exp_done prob_ready nmax_ready nmax_dec mem_scaled settled_sp settled_pool settled_act settled_dve settled_pe stage_free stage_sent
            kv_sent k_sent dec_zeroed k_turned k_copied scores_done q_placed dec_exp p_scaled p_turned p_placed
            raw_used o_copied o_turned o_hi o_placed a_step v_step gain_loaded ms_made ms_read y_turned y_made y_sent""".split()
        S = {n: ctx.enter_context(nc.semaphore(n)) for n in names}

        def slot_of(n):
            return (n + N_PRO + (SHIFT if n >= I_ATT + A_WO else 0)) % 4

        def bank(s, b, lo=0, hi=512):
            return psum[:, (2 * s + b) * 512 + lo:(2 * s + b) * 512 + hi]

        def slot(s):
            return psum[:, s * 1024:(s + 1) * 1024]

        def tok(s):
            return slot(s).rearrange("p (b t) -> p b t", b=2)[:, :, 0:HT]

        def two(ap):
            return ap.rearrange("p (b t) -> p b t", b=2)

        def samples(ap, off, n):
            return ap[:, off:off + NB * n].rearrange("p (b t) -> p b t", b=NB)

        def diag(blk, c):
            return blk[:, c * 1024:c * 1024 + 1152].rearrange("p (e s) -> p e s", s=144)[:, :, 0:16]

        def raw_half(h):
            return raw[:, (h // 2) % 2, :].rearrange("p (k n) -> p k n", n=256)[:, :, (h % 2) * P:(h % 2 + 1) * P]

        def w_half(a, h):
            return W[:, a, h % 4, :].rearrange("p (k n) -> p k n", n=P)

        def done_value(l, n):
            return l * N_LAYER + (N_PRO + n + 1)

        def hidden(a, q):
            return H[:, a, q, :] if isinstance(q, int) else H[:, a, ds(q, 1), :].rearrange("p a t -> p (a t)")

        def dec_cols(a, c, n):
            return (a[:, :, TP + n * 32:TP + (n + 1) * 32] if isinstance(n, int) else a[:, :, ds(n * 32 + TP, 32)])\
                .rearrange("p (h c) (b t) -> p c b h t", c=2, b=2)[:, c]

        block = ctx.enter_context(nc.Block())

        @block.sync
        def _(sp):
            c = Counts(sp, S, S["settled_sp"], True)
            sp.dma_start(mem_rows, mem_prompt[0].rearrange("(c p) d -> p c d", p=P)).then_inc(S["mem_loaded"], 16)
            for t in range(5):
                src = x_prompt[0, t * P:(t + 1) * P, :] if t < 4 else x_sample.rearrange("b t d -> (b t) d")
                sp.dma_start(Mf[:, t * D:(t + 1) * D], src).then_inc(S[f"x_loaded{t}"], 16)
            sp.wait_ge(S["x_loaded2"], 16)

            def load(u, ap, k=KC):
                sp.dma_start(raw[:, u, 0:k * 256].rearrange("p (k n) -> p k n", n=256),
                             ap.rearrange("a (k p) n -> p (a k) n", p=P)).then_inc(S[f"raw_full{u}"], 16)
                c.note(f"raw_full{u}", 16)

            def freed():
                c.take("w_ready", 2)

            def w_in(l, w, col):
                return ffn_w_in[ds(l, 1), w, :, ds(col, 256)]

            load(0, w_in(0, 0, 0))
            load(1, w_in(0, 0, DFF))

            def ffn_loads(l, w):
                for g, (k, g0) in enumerate(zip(GROUPS, GSTART)):
                    with c.loop(1 if w == 0 and g == 0 else 0, k // 2, GROW_BLOCKS) as i:
                        for u in range(2):
                            freed()
                            load(u, w_in(l, w, i * 256 + (g0 * P + u * DFF)))
                    with c.loop(0, 2, GROW_BLOCKS) as i:
                        for u in range(2):
                            freed()
                            load(u, ffn_w_out[ds(l, 1), w, g0 * P:(g0 + k) * P, ds(i * 512 + u * 256, 256)], k)

            def matrix_loads(l, m, pairs):
                with c.loop(0, pairs, GROW_BLOCKS) as i:
                    for u in range(2):
                        freed()
                        load(u, m[ds(l, 1), :, ds(i * 512 + u * 256, 256)])

            def cached(cache, l, b, u):
                sp.dma_start(raw[:, u, :].rearrange("p (c d) -> p c d", c=2),
                             cache[ds(l, 1), ds(b, 1), :, :, :].rearrange("a b (c p) h d -> p (a b c) (h d)", p=P))\
                    .then_inc(S[f"raw_full{u}"], 16)
                c.note(f"raw_full{u}", 16)

            with c.loop(0, DEPTH, GROW_LAYER) as l:
                ffn_loads(l, 0)
                for n, col in enumerate((6, 2, 7, 4, 0, 3, 5, 1)):
                    freed()
                    load(n % 2, mix_w_in[ds(l, 1), :, col * 256:(col + 1) * 256])
                matrix_loads(l, mix_w_out, 2)
                matrix_loads(l, wq, 2)
                matrix_loads(l, wkv, 4)
                for u in range(2):
                    freed()
                    load(u, wo[ds(l, 1), :, u * 256:(u + 1) * 256])
                for u in range(2):
                    freed()
                    cached(cache_k, l, u, u)
                for u in range(2):
                    c.take("k_turned", 2)
                    cached(cache_k, l, 2 + u, u)
                with c.loop(0, 2, GROW_PAIR) as n:
                    for u in range(2):
                        c.take("k_turned", 2)
                        cached(cache_v, l, n * 2 + u, u)
                    for u in range(2):
                        c.take("raw_used")
                        cached(cache_k, l, n * 2 + (4 + u), u)
                for u in range(2):
                    c.take("k_turned", 2)
                    cached(cache_v, l, 4 + u, u)
                for u in range(2):
                    c.take("raw_used")
                    cached(cache_v, l, 6 + u, u)
                for u in range(2):
                    c.take("raw_used")
                    load(u, wo[ds(l, 1), :, (2 + u) * 256:(3 + u) * 256])
                ffn_loads(l, 1)
                for u in range(2):
                    freed()
                    load(u, w_in(1 - l, 0, u * DFF))

        @block.gpsimd
        def _(pool):
            c = Counts(pool, S, S["settled_pool"], True)
            nc.gpsimd.memset(ident[:, :], 0.0).then_inc(S["consts"], 1)
            pool.wait_ge(S["consts"], 1)
            nc.gpsimd.affine_select(out=ident[:, :], in_=ident[:, :], compare_op=ALU.not_equal, fill=1.0,
                                    base=0, pattern=[[-1, P]], channel_multiplier=1).then_inc(S["consts"], 1)
            nc.gpsimd.memset(onesd[:, :], 1.0 / D).then_inc(S["consts"], 1)
            for t in range(PS):
                nc.gpsimd.memset(invc[:, t:t + 1], 1.0 / (t + 1)).then_inc(S["counts_made"], 1)
            pool.wait_ge(S["mem_rstd"], 1)
            for i in range(2):
                nc.gpsimd.tensor_scalar(mem_rows[:, i, :], mem_rows[:, i, :], small[:, 2 + i:3 + i], None,
                                        ALU.mult).then_inc(S["mem_scaled"], 1)
            pool.sem_inc(S["stage_free"], 1)

            def sent(l, n, s_out, p_out, col, rows):
                def end(b):
                    return (b % 4 + 1) * (rows + 16)

                pool.wait_ge(S["item_done"], done_value(l, n))
                c.settle()
                for b in range(NB):
                    pool.dma_start(s_out[ds(l, 1), b, :, col:col + 256].rearrange("a t f -> (a t) f"),
                                   stage[end(b) - rows:end(b), b // 4, :]).then_inc(S["stage_sent"], 16)
                pool.dma_start(p_out[ds(l, 1), :, :, col:col + 256].rearrange("a b t f -> (a b t) f"),
                               stage[16 - rows:16, 2, :]).then_inc(S["stage_sent"], 16)
                c.take("stage_sent", 16 * (NB + 1))
                pool.sem_inc(S["stage_free"], 1)

            with c.loop(0, DEPTH, GROW_LAYER) as l:
                for j in range(2):
                    sent(l, I_MIX + M_SP[j], pool_s_out, pool_p_out, j * 256, PS)
                for j in range(2):
                    sent(l, I_MIX + M_SC[j], conv_s_out, conv_p_out, j * 256, 2)
                pool.wait_ge(S["hid_ready"], l * GROW_LAYER["hid_ready"] + HID_Q)
                c.settle()
                nc.gpsimd.memset(qblk, 0.0).then_inc(S["dec_zeroed"], 1)
                for items, out, i0 in ((A_KB, mem_k_out, 0), (A_VB, mem_v_out, 2)):
                    for h in range(NH):
                        pool.wait_ge(S["item_done"], done_value(l, I_ATT + items[h]))
                        c.settle()
                        pool.dma_start(out[ds(l, 1), 0, :, h, :].rearrange("a (c p) d -> p (a c) d", p=P),
                                       kv_st[i0 + h % 2]).then_inc(S["kv_sent"], 16)
                        c.take("kv_sent", 16)
                        pool.sem_inc(S["k_sent"], 1)
                nc.gpsimd.memset(pblk, 0.0).then_inc(S["dec_zeroed"], 1)
            pool.wait_ge(S["item_done"], done_value(DEPTH - 1, I_FFN[1]))
            pool.dma_start(gain_row, final_norm.partition_broadcast(P)).then_inc(S["gain_loaded"], 16)

        @block.scalar
        def _(act):
            c = Counts(act, S, S["settled_act"])

            def split(h):
                if h % 2 == 0:
                    c.take(f"raw_full{(h // 2) % 2}", 16)
                c.own()
                nc.scalar.activation(w_half(0, h), raw_half(h), ACT.Copy).then_inc(S["w_hi"], 1)
                c.did("w_hi")

            def hi_part(m, gcol):
                c.own()
                nc.scalar.activation(X[:, 0, m, :], xT[:, m, :], ACT.Copy, scale=parl[:, gcol + m:gcol + m + 1])\
                    .then_inc(S["xn_hi"], 1)
                c.did("xn_hi")

            def square(m):
                c.own()
                nc.scalar.activation(sqsum[:, :] if m == 0 else sq[m % 2], xT[:, m, :], ACT.Square)\
                    .then_inc(S["x_sq"], 1)
                c.did("x_sq")

            def norm_part(m, gcol):
                hi_part(m, gcol)
                square(m)

            def rms():
                c.take("item_ready")
                c.note("item_done")
                c.take("recip_done")
                c.own()
                nc.scalar.activation(rstd[:, :], sqsum[:, :], ACT.Sqrt).then_inc(S["rstd_ready"], 1)
                c.did("rstd_ready")

            def hidden_hi(out, v):
                c.take("hid_f32")
                c.own()
                nc.scalar.activation(out, v, ACT.Copy).then_inc(S["hid_hi"], 1)
                c.did("hid_hi")

            for r0, src in parameter_rows(ffn_norm, mix_norm, xattn_norm, mem_norm, pool_scale, conv_w, final_norm):
                act.dma_start(mrow[r0:r0 + src.shape[0], 0, 0:P], src).then_inc(S["rows_loaded"], 16)
            act.wait_ge(S["mem_loaded"], 16)
            for i in range(2):
                c.own()
                nc.scalar.activation(Mf[:, 5 * D:6 * D], mem_rows[:, i, :], ACT.Square,
                                     accum_out=small[:, i:i + 1]).then_inc(S["mem_sq"], 1)
                c.did("mem_sq")
            act.wait_ge(S["mem_ms"], 1)
            c.own()
            nc.scalar.activation(small[:, 2:4], small[:, 2:4], ACT.Sqrt).then_inc(S["mem_rstd"], 1)
            c.did("mem_rstd")
            for t in (1, 3):
                act.wait_ge(S["item_ready"], t + 2)
                c.own()
                nc.scalar.activation(xT[:, :, t * P:(t + 1) * P], slot((t + 1) % 4).rearrange("p (k t) -> p k t", k=KC),
                                     ACT.Copy).then_inc(S["x_copied"], 1)
                c.did("x_copied")
            c.note("item_ready", N_PRO)
            c.take("item_done", 6)
            c.note("item_done", 2)
            c.take("par_ready")
            for m in range(KC):
                hi_part(m, G_FFN[0])
                if m % 4 == 1:
                    split(m // 4)
            for m in range(KC):
                if m >= 3:
                    act.wait_ge(S["sq_added"], m - 2)
                square(m)
            split(2)
            split(3)

            def gate_up(q, h0, first):
                for e in range(2):
                    c.take("item_ready")
                    if first and e == 0:
                        rms()
                    c.take("item_done")
                    c.own()
                    nc.scalar.activation(gate[e], gate[e], ACT.Silu).then_inc(S["gate_silu"], 1)
                    c.did("gate_silu")
                    split(h0 + 4 + e)
                for e in range(2):
                    c.take("item_ready")
                    c.note("item_done")
                    hidden_hi(hidden(0, q(e)), val[e])
                    split(h0 + 6 + e)

            def update(m, h, gcol=None):
                c.take("item_ready")
                c.take("item_done")
                if gcol is not None:
                    norm_part(m, gcol)
                split(h + 4)

            def ffn(w):
                h = (H_FFN0, H_FFN1)[w]
                for g, k in enumerate(GROUPS):
                    n = k // 2
                    if g == 0:
                        gate_up(lambda e: e, h, True)
                        n, h = n - 1, h + 4
                    with c.loop(0, n, GROW_IN) as i:
                        gate_up(lambda e: i * 2 + (2 * (g == 0) + e), h, False)
                    h += 4 * n
                    if g < 2:
                        with c.loop(0, 2, GROW_OUT) as i:
                            for m in range(4):
                                update(None, h + m)
                    else:
                        for m in range(KC):
                            update(m, h + m, (G_MIX, G_NEXT)[w])
                    h += KC

            with c.loop(0, DEPTH, GROW_LAYER) as l:
                c.own()
                act.dma_start(mrow[:, 0, :].rearrange("p (g d) -> p g d", g=4),
                              pool_w[ds(l, 1)].rearrange("a g c d -> c (a g) d")).then_inc(S["misc_loaded"], 16)
                act.dma_start(mrow[0:NB * PS, 1, :], state_pool[ds(l, 1)].rearrange("a b t f -> (a b t) f"))\
                    .then_inc(S["misc_loaded"], 16)
                act.dma_start(mrow[0:NB * 2, 2, :], state_conv[ds(l, 1)].rearrange("a b t f -> (a b t) f"))\
                    .then_inc(S["misc_loaded"], 16)
                c.take("par_ready")
                ffn(0)

                c.take("misc_loaded", 48)
                c.own()
                nc.scalar.activation(pw[:, 0, :, :], mrow[:, 0, :].rearrange("p (g f) -> p g f", g=4), ACT.Copy)\
                    .then_inc(S["pw_hi"], 1)
                c.did("pw_hi")
                c.take("item_ready")
                c.note("item_done")
                h = H_MIX
                for kind, e in MIX_STEPS:
                    c.take("item_ready")
                    if (kind, e) == ("P", 0):
                        rms()
                    n = I_MIX + (M_PW[e] if kind == "W" else 0)
                    if kind == "W":
                        c.own()
                        nc.scalar.activation(two(H[:, 0, 4 + e, :]), tok(slot_of(n)), ACT.Copy,
                                             scale=parl[:, G_PSCALE + e:G_PSCALE + e + 1]).then_inc(S["part_hi"], 1)
                        c.did("part_hi")
                    c.note("item_done")
                    if kind == "P":
                        hidden_hi(H[:, 0, 4 + e, :], val[e % 2])
                    if kind == "B":
                        hidden_hi(H[:, 0, e, :], val[e % 2])
                    if kind in "PCVB":
                        split(h + 4)
                        h += 1
                for m in range(KC):
                    update(m, h + m, G_ATT)

                def mem_hi():
                    for k in range(KC):
                        c.own()
                        nc.scalar.activation(memx[:, 0, k, :], memT[:, k, :], ACT.Copy,
                                             scale=parl[:, G_MEM + k:G_MEM + k + 1]).then_inc(S["part_hi"], 1)
                        c.did("part_hi")

                for m in range(KC):
                    c.take("item_ready")
                    if m == 0:
                        rms()
                    if m == KC - 1:
                        mem_hi()
                    c.take("item_done")
                    c.own()
                    nc.scalar.activation(H[:, 0, m, :], val[m % 2], ACT.Copy).then_inc(S["hid_hi"], 1)
                    c.did("hid_hi")
                    split(H_Q + 4 + m)

                def part_hi(out, in_):
                    c.own()
                    nc.scalar.activation(out, in_, ACT.Copy).then_inc(S["part_hi"], 1)
                    c.did("part_hi")

                h = H_KV
                for kind, e in ATT_STEPS:
                    c.take("item_ready")
                    n = dict(K=A_KB, k=A_TK, V=A_VB, S=A_S, T=A_TP, O=A_PV)[kind][e]
                    s = slot_of(I_ATT + n)
                    if kind == "k":
                        part_hi(KTp[:, 0, 2 * e:2 * e + 2, :], bank(s, 0).rearrange("p (c m) -> p c m", c=2))
                    if kind == "V":
                        if e >= 2:
                            c.take("k_sent", 5 if e == 2 else 1)
                        c.own()
                        nc.scalar.activation(kv_st[2 + e % 2], two(slot(s))[:, :, 0:256], ACT.Copy)\
                            .then_inc(S["a_step"], 1)
                        c.did("a_step")
                        part_hi(Vp[0][:, :, e * 256:(e + 1) * 256], two(slot(s))[:, :, 0:256])
                    if kind == "S":
                        c.take("nmax_ready")
                        for t in range(4):
                            c.own()
                            last = "exp_done" if t == 3 else "a_step"
                            o = 4 + 16 * (e % 2)
                            nc.scalar.activation(prob[e % 2][:, t, :], slot(s)[:, t * 256:(t + 1) * 256], ACT.Exp,
                                                 bias=small[:, o + t:o + t + 1], scale=1.0 / 16,
                                                 accum_out=small[:, o + 4 + t:o + 5 + t]).then_inc(S[last], 1)
                            c.did(last)
                    if kind == "T":
                        part_hi(PT[e % 2][:, 0, :, :], two(slot(s)))
                    if kind == "O":
                        part_hi(H[:, 0, 2 * e:2 * e + 2, 0:TP], two(slot(s)))
                    c.note("item_done")
                    if kind in "KV" and (kind, e) not in LATE.values() or (kind, e) in LATE:
                        split(h + 4)
                        split(h + 5)
                        h += 2

                c.take("dec_zeroed", 2)

                def copy_keys(first):
                    for j in range(4):
                        c.take("k_turned")
                        if not (first and j < 2):
                            c.take("scores_done")
                        c.own()
                        nc.scalar.activation(k_dec[j % 2], slot(KEY_SLOTS[j % 2]), ACT.Copy).then_inc(S["k_copied"], 1)
                        c.did("k_copied")

                def exps():
                    c.take("nmax_dec")
                    c.own()
                    nc.scalar.activation(p_dec, bank(SCORE_SLOT, 0, 0, 256), ACT.Exp, bias=small[:, 40:41], scale=1.0 / 16,
                                         accum_out=small[:, 41:42]).then_inc(S["dec_exp"], 1)
                    c.did("dec_exp")

                def output_hi(n):
                    c.take("o_turned")
                    for i in range(2):
                        c.own()
                        last = "o_hi" if i else "a_step"
                        nc.scalar.activation(dec_cols(H[:, 0], i, n),
                                             bank(OUT_SLOT, 0, i * P, (i + 1) * P).rearrange("p (b h t) -> p b h t", b=2, h=4),
                                             ACT.Copy).then_inc(S[last], 1)
                        c.did(last)

                copy_keys(True)
                exps()
                with c.loop(0, 3, GROW_PAIR) as n:
                    copy_keys(False)
                    exps()
                    output_hi(n)
                output_hi(3)
                c.note("k_sent", 2)
                c.note("scores_done", 2)
                c.note("raw_full0", 8 * 16)
                c.note("raw_full1", 8 * 16)
                for m in range(KC):
                    update(m, H_WO + m, G_FFN[1])
                ffn(1)

            act.wait_ge(S["ms_read"], 2)
            c.own()
            nc.scalar.activation(small[:, 0:5], small[:, 0:5], ACT.Sqrt).then_inc(S["rstd_ready"], 1)
            for t in range(5):
                act.wait_ge(S["y_made"], t + 1)
                dst = y_prompt[0, t * P:(t + 1) * P, :] if t < 4 else y_sample.rearrange("b t d -> (b t) d")
                act.dma_start(dst, Mf[:, t * D:(t + 1) * D]).then_inc(S["y_sent"], 16)
            act.wait_ge(S["y_sent"], 80)

        @block.vector
        def _(dve):
            c = Counts(dve, S, S["settled_dve"])
            TT = nc.vector.tensor_tensor

            def step(name="v_step"):
                c.own()
                c.did(name)
                return S[name]

            def split(h):
                c.take("w_hi")
                s = step("w_ready")
                TT(w_half(1, h), raw_half(h), w_half(0, h).bitcast(f32), ALU.subtract).then_inc(s, 1)

            def lo_only(m, gcol):
                c.take("xn_hi")
                s = step("xn_ready")
                nc.vector.scalar_tensor_tensor(out=X[:, 1, m, :], in0=xT[:, m, :],
                                               scalar=parl[:, gcol + m:gcol + m + 1],
                                               in1=X[:, 0, m, :].bitcast(f32), op0=ALU.mult,
                                               op1=ALU.subtract).then_inc(s, 1)

            def add_square(m):
                c.take("x_sq")
                if m:
                    s = step("sq_added")
                    TT(sqsum[:, :], sqsum[:, :], sq[m % 2], ALU.add).then_inc(s, 1)

            def lo_part(m, gcol):
                lo_only(m, gcol)
                add_square(m)

            def rms(n):
                s = step("item_done")
                nc.vector.tensor_scalar(two(sqsum[:, :]), tok(slot_of(n)), EPS, None, ALU.add).then_inc(s, 1)
                s = step("recip_done")
                nc.vector.reciprocal(sqsum[:, :], sqsum[:, :]).then_inc(s, 1)

            def scaled(out, n):
                s = step("item_done")
                TT(two(out), tok(slot_of(n)), two(rstd[:, :]), ALU.mult).then_inc(s, 1)

            def hidden_lo(chunk, v):
                c.take("hid_hi")
                s = step("hid_ready")
                TT(hidden(1, chunk), v, hidden(0, chunk).bitcast(f32), ALU.subtract).then_inc(s, 1)

            dve.wait_ge(S["mem_sq"], 2)
            s = step("v_step")
            nc.vector.tensor_scalar(small[:, 2:4], small[:, 0:2], 1.0 / D, EPS, ALU.mult, ALU.add).then_inc(s, 1)
            s = step("mem_ms")
            nc.vector.reciprocal(small[:, 2:4], small[:, 2:4]).then_inc(s, 1)
            dve.wait_ge(S["item_ready"], 1)
            s = step("item_done")
            nc.vector.tensor_copy(par[:, :], bank(0, 0, 0, N_PAR)).then_inc(s, 1)
            s = step("par_ready")
            nc.vector.tensor_copy(parl[:, 0:KC], par[:, 0:KC]).then_inc(s, 1)
            for t in range(5):
                if t % 2:
                    continue
                dve.wait_ge(S["item_ready"], t + 2)
                s = step("item_done")
                nc.vector.tensor_copy(xT[:, :, t * P:(t + 1) * P],
                                      slot((t + 1) % 4).rearrange("p (k t) -> p k t", k=KC)).then_inc(s, 1)
            dve.wait_ge(S["x_copied"], 2)
            c.own()
            dve.sem_inc(S["item_done"], 2)
            c.note("item_done", 2)
            for m in range(KC):
                lo_only(m, G_FFN[0])
                if m % 4 == 1:
                    split(m // 4)
            dve.wait_ge(S["item_ready"], N_PRO)
            for i in range(2):
                s = step("item_done")
                nc.vector.tensor_copy(memT[:, :, i * P:(i + 1) * P],
                                      slot(2 + i).rearrange("p (k t) -> p k t", k=KC)).then_inc(s, 1)
                if i == 0:
                    for m in range(KC):
                        add_square(m)
            split(2)
            split(3)
            dve.wait_ge(S["counts_made"], PS)
            c.n["item_ready"] = N_PRO

            def first_item(n):
                c.take("item_ready", 2)
                rms(n)
                c.take("rstd_ready")

            def gate_up(q, n, h0, first):
                for e in range(2):
                    if first and e == 0:
                        first_item(n - 1)
                    else:
                        c.take("item_ready")
                    scaled(gate[e], n + e)
                    split(h0 + 4 + e)
                for e in range(2):
                    c.take("item_ready")
                    scaled(val[e], n + 2 + e)
                    c.take("gate_silu")
                    s = step("hid_f32")
                    TT(val[e], val[e], gate[e], ALU.mult).then_inc(s, 1)
                    hidden_lo(q(e), val[e])
                    split(h0 + 6 + e)

            def update(m, n, h, scale, gcol=None):
                c.take("item_ready")
                s = step("item_done")
                x = xT[:, m, :].rearrange("p a (b t) -> p (a b) t", b=2) if not isinstance(m, int) else two(xT[:, m, :])
                nc.vector.scalar_tensor_tensor(out=x, in0=tok(slot_of(n)), scalar=scale, in1=x, op0=ALU.mult,
                                               op1=ALU.add).then_inc(s, 1)
                if gcol is not None:
                    lo_part(m, gcol)
                split(h + 4)

            def ffn(w):
                h = (H_FFN0, H_FFN1)[w]
                for g, k in enumerate(GROUPS):
                    n, it = I_FFN[w] + FFN_IN[g], k // 2
                    if g == 0:
                        gate_up(lambda e: e, n, h, True)
                        n, it, h = n + 4, it - 1, h + 4
                    with c.loop(0, it, GROW_IN) as i:
                        gate_up(lambda e: i * 2 + (2 * (g == 0) + e), n, h, False)
                    h += 4 * it
                    n = I_FFN[w] + FFN_OUT[g]
                    if g < 2:
                        with c.loop(0, 2, GROW_OUT) as i:
                            for m in range(4):
                                update(ds(i * 4 + m, 1), n + m, h + m, 0.5)
                    else:
                        for m in range(KC):
                            update(m, n + m, h + m, 0.5, (G_MIX, G_NEXT)[w])
                    h += KC

            with c.loop(0, DEPTH, GROW_LAYER) as l:
                s = step()
                nc.vector.tensor_copy(parl[:, 0:G_MIX], par[:, ds(l * 2 * KC, 3 * KC)]).then_inc(s, 1)
                for g, r in zip((G_MIX, G_ATT, G_MEM), range(R_GAINS, R_PSCALE, 2 * KC)):
                    s = step()
                    nc.vector.tensor_copy(parl[:, g:g + KC], par[:, ds(l * KC + r, KC)]).then_inc(s, 1)
                s = step()
                nc.vector.tensor_copy(parl[:, G_PSCALE:G_CONV], par[:, ds(l * 4 + R_PSCALE, 4)]).then_inc(s, 1)
                s = step("par_ready")
                nc.vector.tensor_copy(parl[:, G_CONV:], par[:, ds(l * 12 + R_CONV, 12)]).then_inc(s, 1)
                ffn(0)

                I = I_MIX
                c.take("pw_hi")
                s = step("pw_ready")
                TT(pw[:, 1, :, :], mrow[:, 0, :].rearrange("p (g f) -> p g f", g=4), pw[:, 0, :, :].bitcast(f32),
                   ALU.subtract).then_inc(s, 1)
                c.take("item_ready")
                s = step()
                nc.vector.tensor_copy(Mf[:, 5448:5928], bank(slot_of(I), 0, 0, 480)).then_inc(s, 1)
                s = step("item_done")
                nc.vector.tensor_copy(Mf[:, 5928:5992], bank(slot_of(I), 1, 0, 64)).then_inc(s, 1)

                def prefixed(ext, e, pfx, n):
                    s = step()
                    nc.vector.memset(ext[:, 0:n], 0.0).then_inc(s, 1)
                    s = step()
                    nc.vector.tensor_copy(samples(ext, n + TP, n + 16)[:, :, 0:n], pfx[:, e, :, :]).then_inc(s, 1)

                def pooled(e):
                    w = 2 << e
                    p, n = p_ext[e % 2], I + M_P[e]
                    prefixed(p, e, pfx_pool, PS)
                    r = rstd
                    s_ = slot_of(n)
                    s = step()
                    TT(p[:, PS:PS + HT], bank(s_, 0, 0, HT), r[:, 0:HT], ALU.mult).then_inc(s, 1)
                    s = step()
                    TT(p[:, PS + HT:PS + TP], bank(s_, 1, 0, TP - HT), r[:, HT:TP], ALU.mult).then_inc(s, 1)
                    s = step("item_done")
                    TT(samples(p, PS + TP, PS + 16)[:, :, PS:], samples(bank(s_, 1), TP - HT, 16),
                       samples(r, TP, 16), ALU.mult).then_inc(s, 1)
                    src, size = p, PX
                    for k in range(e + 1):
                        size -= 1 << k
                        s = step()
                        TT(sums[k % 2][:, 0:size], src[:, 0:size], src[:, (1 << k):(1 << k) + size],
                           ALU.add).then_inc(s, 1)
                        src = sums[k % 2]
                    v = val[e % 2]
                    o = PS - (w - 1)
                    s = step()
                    nc.vector.scalar_tensor_tensor(
                        out=samples(v, TP, 16), in0=samples(src, PS + TP, PS + 16)[:, :, o:o + 16],
                        scalar=1.0 / w, in1=samples(p, PS + TP, PS + 16)[:, :, PS:],
                        op0=ALU.mult, op1=ALU.subtract).then_inc(s, 1)
                    s = step()
                    nc.vector.scalar_tensor_tensor(out=v[:, w - 1:TP], in0=src[:, PS:PS + TP - w + 1],
                                                   scalar=1.0 / w, in1=p[:, PS + w - 1:PS + TP],
                                                   op0=ALU.mult, op1=ALU.subtract).then_inc(s, 1)
                    s = step()
                    TT(v[:, 0:w - 1], src[:, o:o + w - 1], invc[:, 0:w - 1], ALU.mult).then_inc(s, 1)
                    s = step("hid_f32")
                    TT(v[:, 0:w - 1], v[:, 0:w - 1], p[:, PS:PS + w - 1], ALU.subtract).then_inc(s, 1)
                    hidden_lo(4 + e, v)

                def state_rows(n, rows):
                    c.take("stage_free")
                    s_ = slot_of(n)
                    s = step()
                    r = 4 * (rows + 16)
                    nc.vector.tensor_copy(stage[0:r, 0:2, :], two(bank(s_, 0))[0:r]).then_inc(s, 1)
                    s = step("item_done")
                    nc.vector.tensor_copy(stage[0:16, 2, :], bank(s_, 1, 0, 256)[0:16, :]).then_inc(s, 1)

                def conv(e):
                    u, n = u_ext[e % 2], I + M_V[e]
                    scaled(val[e % 2], n)
                    prefixed(u, e, pfx_conv, 2)
                    s = step()
                    TT(u[:, 2:2 + TP], val[e % 2][:, 0:TP], gate[e % 2][:, 0:TP], ALU.mult).then_inc(s, 1)
                    s = step("v_step")
                    TT(samples(u, 2 + TP, 18)[:, :, 2:], samples(val[e % 2], TP, 16), samples(gate[e % 2], TP, 16),
                       ALU.mult).then_inc(s, 1)
                    t = taps[e % 2][:, 0:UX - 2]
                    for k in range(CW):
                        col = parl[:, G_CONV + 4 * k + e:G_CONV + 4 * k + e + 1]
                        s = step()
                        if k == 0:
                            nc.vector.tensor_scalar(t, u[:, 0:UX - 2], col, None, ALU.mult).then_inc(s, 1)
                        else:
                            nc.vector.scalar_tensor_tensor(out=t, in0=u[:, k:k + UX - 2], scalar=col, in1=t,
                                                           op0=ALU.mult, op1=ALU.add).then_inc(s, 1)

                def gated(e):
                    v, t = val[e % 2], taps[e % 2]
                    scaled(v, I + M_B[e])
                    s = step()
                    TT(v[:, 0:TP], v[:, 0:TP], t[:, 0:TP], ALU.mult).then_inc(s, 1)
                    s = step("hid_f32")
                    TT(samples(v, TP, 16), samples(v, TP, 16), samples(t, 2 + TP, 18)[:, :, 0:16],
                       ALU.mult).then_inc(s, 1)
                    hidden_lo(e, v)

                h = H_MIX
                for kind, e in MIX_STEPS:
                    if (kind, e) == ("P", 0):
                        first_item(I + 1)
                    elif (kind, e) == ("P", 2):
                        c.take("item_ready", 2)
                    elif (kind, e) != ("p", 0):
                        c.take("item_ready")
                    if kind == "P":
                        pooled(e)
                    elif kind == "p":
                        state_rows(I + M_SP[e], PS)
                    elif kind == "C":
                        scaled(gate[e % 2], I + M_C[e])
                    elif kind == "V":
                        conv(e)
                    elif kind == "B":
                        gated(e)
                    elif kind == "c":
                        state_rows(I + M_SC[e], 2)
                    elif kind == "W":
                        c.take("part_hi")
                        s = step("item_done")
                        nc.vector.scalar_tensor_tensor(out=two(H[:, 1, 4 + e, :]), in0=tok(slot_of(I + M_PW[e])),
                                                       scalar=parl[:, G_PSCALE + e:G_PSCALE + e + 1],
                                                       in1=two(Hf[:, 0, 4 + e, :]), op0=ALU.mult,
                                                       op1=ALU.subtract).then_inc(s, 1)
                    if kind in "PCVB":
                        split(h + 4)
                        h += 1
                for m in range(KC):
                    update(m, I + M_OUT + m, h + m, 1.0, G_ATT)

                def place_queries(n):
                    for i in range(2):
                        s = step("q_placed" if i else "v_step")
                        TT(diag(qblk, i).rearrange("p (b h) t -> p b h t", b=2), dec_cols(Hf[:, 0], i, n),
                           dec_cols(Hf[:, 1], i, n), ALU.add).then_inc(s, 1)

                def mem_lo():
                    for k in range(KC):
                        c.take("part_hi")
                        s = step("memx_ready")
                        nc.vector.scalar_tensor_tensor(out=memx[:, 1, k, :], in0=memT[:, k, :],
                                                       scalar=parl[:, G_MEM + k:G_MEM + k + 1],
                                                       in1=memx[:, 0, k, :].bitcast(f32), op0=ALU.mult,
                                                       op1=ALU.subtract).then_inc(s, 1)

                I = I_ATT
                for m in range(KC):
                    if m == 0:
                        first_item(I)
                    else:
                        c.take("item_ready")
                    scaled(val[m % 2], I + A_Q + m)
                    if m == KC - 1:
                        mem_lo()
                    hidden_lo(m, val[m % 2])
                    split(H_Q + 4 + m)
                def scale_probabilities(e):
                    o = 4 + 16 * (e % 2)
                    for t in range(4):
                        s = step("prob_ready" if t == 3 else "v_step")
                        nc.vector.tensor_scalar(prob[e % 2][:, t, :], prob[e % 2][:, t, :],
                                                small[:, o + 8 + t:o + 9 + t], None, ALU.mult).then_inc(s, 1)

                h = H_KV
                for kind, e in ATT_STEPS:
                    if (kind, e) == ("T", 3):
                        c.take("dec_zeroed")
                        place_queries(0)
                    c.take("item_ready")
                    s_ = slot_of(I + dict(K=A_KB, k=A_TK, V=A_VB, S=A_S, T=A_TP, O=A_PV)[kind][e])
                    if kind == "K":
                        if e >= 2:
                            c.take("k_sent")
                        s = step("item_done")
                        nc.vector.tensor_copy(kv_st[e % 2], two(slot(s_))[:, :, 0:256]).then_inc(s, 1)
                    elif kind == "k":
                        c.take("part_hi")
                        s = step("item_done")
                        TT(KTp[:, 1, 2 * e:2 * e + 2, :], bank(s_, 0).rearrange("p (c m) -> p c m", c=2),
                           KTp[:, 0, 2 * e:2 * e + 2, :].bitcast(f32), ALU.subtract).then_inc(s, 1)
                    elif kind == "V":
                        c.take("part_hi")
                        s = step("item_done")
                        TT(Vp[1][:, :, e * 256:(e + 1) * 256], two(slot(s_))[:, :, 0:256],
                           Vp[0][:, :, e * 256:(e + 1) * 256].bitcast(f32), ALU.subtract).then_inc(s, 1)
                    elif kind == "S":
                        o = 4 + 16 * (e % 2)
                        s = step()
                        nc.vector.tensor_reduce(small[:, o + 12:o + 16], slot(s_).rearrange("p (t m) -> p t m", t=4),
                                                axis=AX.X, op=ALU.max).then_inc(s, 1)
                        s = step("nmax_ready")
                        nc.vector.tensor_scalar(small[:, o:o + 4], small[:, o + 12:o + 16], -1.0 / 16, None,
                                                ALU.mult).then_inc(s, 1)
                        if e % 2:
                            scale_probabilities(e - 1)
                        c.take("exp_done")
                        s = step("item_done")
                        nc.vector.reciprocal(small[:, o + 8:o + 12], small[:, o + 4:o + 8]).then_inc(s, 1)
                        if e % 2:
                            scale_probabilities(e)
                    elif kind == "T":
                        c.take("part_hi")
                        s = step("item_done")
                        TT(PT[e % 2][:, 1, :, :], two(slot(s_)), PT[e % 2][:, 0, :, :].bitcast(f32), ALU.subtract).then_inc(s, 1)
                    elif kind == "O":
                        c.take("part_hi")
                        s = step("item_done")
                        TT(H[:, 1, 2 * e:2 * e + 2, 0:TP], two(slot(s_)), Hf[:, 0, 2 * e:2 * e + 2, 0:TP],
                           ALU.subtract).then_inc(s, 1)
                    if kind in "KV" and (kind, e) not in LATE.values() or (kind, e) in LATE:
                        split(h + 4)
                        split(h + 5)
                        h += 2
                c.note("k_sent", 6)

                c.take("dec_zeroed")

                def maxima():
                    c.take("scores_done", 4)
                    s = step()
                    nc.vector.tensor_reduce(small[:, 43:44], bank(SCORE_SLOT, 0, 0, 256), axis=AX.X, op=ALU.max).then_inc(s, 1)
                    s = step("nmax_dec")
                    nc.vector.tensor_scalar(small[:, 40:41], small[:, 43:44], -1.0 / 16, None, ALU.mult)\
                        .then_inc(s, 1)

                def probabilities():
                    c.take("dec_exp")
                    s = step()
                    nc.vector.reciprocal(small[:, 42:43], small[:, 41:42]).then_inc(s, 1)
                    s = step("p_scaled")
                    nc.vector.tensor_scalar(p_dec, p_dec, small[:, 42:43], None, ALU.mult).then_inc(s, 1)

                def place_probabilities():
                    c.take("p_turned")
                    for i in range(2):
                        s = step("p_placed" if i else "v_step")
                        nc.vector.tensor_copy(diag(pblk, i), bank(SCORE_SLOT, 1, i * P, (i + 1) * P)
                                              .rearrange("p (e t) -> p e t", e=8)).then_inc(s, 1)

                def output_lo(n):
                    c.take("o_turned")
                    c.take("o_hi")
                    for i in range(2):
                        s = step("o_placed" if i else "v_step")
                        TT(dec_cols(H[:, 1], i, n), bank(OUT_SLOT, 0, i * P, (i + 1) * P)
                           .rearrange("p (b h t) -> p b h t", b=2, h=4), dec_cols(Hf[:, 0], i, n),
                           ALU.subtract).then_inc(s, 1)

                def copy_output():
                    c.take("raw_used", 2)
                    s = step("o_copied")
                    nc.vector.tensor_copy(o_dec, bank(OUT_SLOT, 1, 0, 256)).then_inc(s, 1)

                maxima()
                place_queries(1)
                probabilities()
                with c.loop(0, 2, GROW_PAIR) as n:
                    place_probabilities()
                    maxima()
                    place_queries(n + 2)
                    probabilities()
                    copy_output()
                    output_lo(n)
                place_probabilities()
                maxima()
                probabilities()
                copy_output()
                output_lo(2)
                place_probabilities()
                copy_output()
                output_lo(3)
                for m in range(KC):
                    update(m, I + A_WO + m, H_WO + m, 1.0, G_FFN[1])
                ffn(1)

            dve.wait_ge(S["ms_made"], 1)
            s = step("ms_read")
            nc.vector.tensor_scalar(small[:, 0:5], bank(3, 0, 0, 5), EPS, None, ALU.add).then_inc(s, 1)
            s = step("ms_read")
            nc.vector.reciprocal(small[:, 0:5], small[:, 0:5]).then_inc(s, 1)
            c.take("rstd_ready")
            dve.wait_ge(S["gain_loaded"], 16)
            for t in range(5):
                dve.wait_ge(S["y_turned"], t + 1)
                s = step("y_made")
                nc.vector.scalar_tensor_tensor(out=Mf[:, t * D:(t + 1) * D], in0=slot(t % 4),
                                               scalar=small[:, t:t + 1], in1=gain_row, op0=ALU.mult,
                                               op1=ALU.mult).then_inc(s, 1)

        @block.tensor
        def _(pe):
            c = Counts(pe, S, S["settled_pe"])
            mm = nc.tensor.matmul

            def three_passes(outs, k, K, lhs, rhs):
                last = None
                for n, (a, b) in enumerate(((0, 0), (0, 1), (1, 0))):
                    for o, out in enumerate(outs):
                        last = mm(out, lhs(a, o), rhs(b, o), start=(k == 0 and n == 0), stop=(k == K - 1 and n == 2))
                return last

            def token_item(n, h, moving, K=KC, ready=None):
                c.take("item_done")
                c.take("w_ready")
                s = slot_of(n)
                for k in range(K):
                    if ready:
                        ready(k)
                    last = three_passes([bank(s, b, 0, HT) for b in range(2)], k, K,
                                        lambda a, o: w_half(a, h)[:, k, :],
                                        lambda a, o: moving[:, a, k, o * HT:(o + 1) * HT])
                last.then_inc(S["item_ready"], 1)
                c.note("item_ready")

            def norm_item(n):
                c.take("sq_added", 7)
                norm_sum(slot_of(n))

            def norm_sum(s):
                for b in range(2):
                    last = mm(bank(s, b, 0, HT), onesd[:, :], sqsum[:, b * HT:(b + 1) * HT], start=True, stop=True)
                last.then_inc(S["item_ready"], 1)
                c.note("item_ready")

            def turn(out, in_, k=P):
                return nc.tensor.transpose(out, in_, ident[0:k, 0:k])

            def chunk_ready(name):
                at = {}

                def ready(k):
                    at.setdefault(k, c.value(name, k + 1))
                    pe.wait_ge(S[name], at[k])
                return ready

            pe.wait_ge(S["consts"], 3)
            pe.wait_ge(S["rows_loaded"], 16 * PARAM_LOADS)
            turn(bank(0, 0, 0, N_PAR), mrow[0:N_PAR, 0, 0:P], N_PAR).then_inc(S["item_ready"], 1)
            for t in range(5):
                pe.wait_ge(S[f"x_loaded{t}"], 16)
                if t >= 3:
                    pe.wait_ge(S["item_done"], t - 2)
                for k in range(KC):
                    last = turn(slot((t + 1) % 4)[:, k * P:(k + 1) * P], Mf[:, t * D + k * P:t * D + (k + 1) * P])
                last.then_inc(S["item_ready"], 1)
            pe.wait_ge(S["mem_scaled"], 2)
            for i in range(2):
                pe.wait_ge(S[("x_copied", "item_done")[i]], (1, 3)[i])
                for k in range(KC):
                    last = turn(slot(2 + i)[:, k * P:(k + 1) * P], mem_rows[:, i, k * P:(k + 1) * P])
                last.then_inc(S["item_ready"], 1)
            pe.wait_ge(S["item_done"], N_PRO - 4)
            c.note("item_ready", N_PRO)
            c.note("item_done", N_PRO - 4)

            def stage_first(n, h):
                c.take("item_done", 1)
                xn = chunk_ready("xn_ready")
                token_item(n + 1, h, X[:, :, :, :], ready=xn)
                c.note("xn_ready", KC)
                norm_item(n)

            def four(n, h, moving, K=KC, ready=None):
                for m in range(4):
                    token_item(n + m, h + m, moving, K, ready if m == 0 else None)

            def ffn(w):
                h = (H_FFN0, H_FFN1)[w]
                for g, k in enumerate(GROUPS):
                    n, it = I_FFN[w] + FFN_IN[g], k // 2
                    if g == 0:
                        stage_first(n - 1, h)
                        for m in range(1, 4):
                            token_item(n + m, h + m, X)
                        n, it, h = n + 4, it - 1, h + 4
                    with c.loop(0, it, GROW_OUT) as i:
                        four(n, h, X)
                    h += 4 * it
                    n = I_FFN[w] + FFN_OUT[g]
                    ready = chunk_ready("hid_ready")
                    with c.loop(0, 2, GROW_OUT) as i:
                        four(n, h, H, k, ready)
                    c.note("hid_ready", k)
                    h += KC

            with c.loop(0, DEPTH, GROW_LAYER) as l:
                ffn(0)

                I, h = I_MIX, H_MIX
                c.take("misc_loaded", 48)
                c.take("item_done")
                s = slot_of(I)
                for g in range(4):
                    turn(bank(s, 0, g * 120, (g + 1) * 120), mrow[0:120, 1, g * P:(g + 1) * P], 120)
                for g in range(4):
                    last = turn(bank(s, 1, g * 16, (g + 1) * 16), mrow[0:16, 2, g * P:(g + 1) * P], 16)
                last.then_inc(S["item_ready"], 1)
                c.note("item_ready")

                def state_item(n, ext, n0, after):
                    c.take("item_done")
                    pe.wait_ge(S[after[0]], after[1])
                    s = slot_of(n)
                    r = 4 * (n0 + 16)
                    for j in range(2):
                        for i in range(2):
                            turn(bank(s, 0, i * 256 + j * P, i * 256 + (j + 1) * P)[0:r],
                                 ext[j][:, n0 + TP + i * r:n0 + TP + (i + 1) * r])
                        last = turn(bank(s, 1, j * P, (j + 1) * P)[0:16, :], ext[j][:, n0 + TP - 16:n0 + TP])
                    last.then_inc(S["item_ready"], 1)
                    c.note("item_ready")

                for kind, e in MIX_STEPS:
                    if (kind, e) == ("P", 0):
                        stage_first(I + 1, h)
                        h += 1
                    elif kind in "PCVB":
                        token_item(I + dict(P=M_P, C=M_C, V=M_V, B=M_B)[kind][e], h, X)
                        h += 1
                    elif kind == "p":
                        state_item(I + M_SP[e], p_ext, PS, ("item_done", done_value(l, I + M_P[2 * e + 1])))
                    elif kind == "c":
                        state_item(I + M_SC[e], u_ext, 2, ("item_done", done_value(l, I + M_B[2 * e])))
                    elif kind == "W":
                        if e == 0:
                            c.take("pw_ready")
                        c.take("item_done")
                        c.take("hid_ready")
                        s = slot_of(I + M_PW[e])
                        three_passes([bank(s, b, 0, HT) for b in range(2)], 0, 1, lambda a, o: pw[:, a, e, :],
                                     lambda a, o: H[:, a, 4 + e, o * HT:(o + 1) * HT]).then_inc(S["item_ready"], 1)
                        c.note("item_ready")
                ya = chunk_ready("hid_ready")

                def y_ready(k):
                    if k < 4:
                        ya(k)
                    elif k == 4:
                        pe.wait_ge(S["item_done"], done_value(l, I + M_PW[3]))
                four(I + M_OUT, h, H, KC, y_ready)
                c.note("hid_ready", 4)
                four(I + M_OUT + 4, h + 4, H)

                I = I_ATT
                stage_first(I, H_Q)
                for m in range(1, KC):
                    token_item(I + A_Q + m, H_Q + m, X)
                mem_chunk = chunk_ready("memx_ready")

                def kv_item(n, h, ready=None):
                    c.take("item_done")
                    c.take("w_ready", 2)
                    s = slot_of(n)
                    for k in range(KC):
                        if ready:
                            ready(k)
                        last = three_passes([bank(s, b, 0, 256) for b in range(2)], k, KC,
                                            lambda a, o: memx[:, a, k, o * P:(o + 1) * P],
                                            lambda a, o: W[:, a, h % 4:h % 4 + 2, :]
                                            .rearrange("p f (k n) -> p f k n", n=P)[:, :, k, :])
                    last.then_inc(S["item_ready"], 1)
                    c.note("item_ready")

                h = H_KV
                for kind, e in ATT_STEPS:
                    if kind in "KV":
                        kv_item(I + (A_KB if kind == "K" else A_VB)[e], h, mem_chunk if (kind, e) == ("K", 0) else None)
                        if (kind, e) == ("K", 0):
                            c.note("memx_ready", KC)
                        h += 2
                        continue
                    c.take("item_done")
                    s = slot_of(I + dict(k=A_TK, S=A_S, T=A_TP, O=A_PV)[kind][e])
                    if kind == "k":
                        pe.wait_ge(S["item_done"], done_value(l, I + A_KB[e]))
                        for i in range(2):
                            for m in range(2):
                                last = turn(bank(s, 0, i * 256 + m * P, i * 256 + (m + 1) * P),
                                            kv_st[e % 2][:, m, i * P:(i + 1) * P])
                    elif kind == "S":
                        pe.wait_ge(S["item_done"], done_value(l, I + A_TK[e]))
                        if e == 0:
                            c.take("hid_ready", KC)
                        for t in range(4):
                            for i in range(2):
                                last = three_passes([slot(s)[:, t * 256:(t + 1) * 256]], i, 2,
                                                    lambda a, o: H[:, a, 2 * e + i, t * P:(t + 1) * P],
                                                    lambda a, o: KTp[:, a, 2 * e + i, :])
                    elif kind == "T":
                        c.take("prob_ready")
                        for t in range(4):
                            for m in range(2):
                                last = turn(bank(s, m, t * P, (t + 1) * P), prob[e % 2][:, t, m * P:(m + 1) * P])
                    elif kind == "O":
                        pe.wait_ge(S["item_done"], done_value(l, I + A_TP[e]))
                        for i in range(2):
                            for m in range(2):
                                last = three_passes([bank(s, i)], m, 2,
                                                    lambda a, o: Vp[a][:, m, e * 256 + i * P:e * 256 + (i + 1) * P],
                                                    lambda a, o: PT[e % 2][:, a, m, :])
                    last.then_inc(S["item_ready"], 1)
                    c.note("item_ready")

                pe.wait_ge(S["item_done"], done_value(l, I + A_TP[3]))

                def turn_keys(j):
                    if j % 2 == 0:
                        c.take(f"raw_full{j // 2}", 16)
                    for k in range(4):
                        for m in range(2):
                            f = (j % 2) * 4 + k
                            last = turn(slot(KEY_SLOTS[j % 2])[:, k * 256 + m * P:k * 256 + (m + 1) * P],
                                        raw[:, j // 2, m * D + f * P:m * D + (f + 1) * P])
                    last.then_inc(S["k_turned"], 1)
                    c.note("k_turned")

                def score(j):
                    c.take("k_copied")
                    for k in range(4):
                        f = (j % 2) * 4 + k
                        e = (j // 2) * 4 + f // 2
                        blk = (f % 2) * 1024 + e * P
                        last = mm(bank(SCORE_SLOT, 0, 0, 256), qblk[:, blk:blk + P], k_dec[j % 2][:, k * 256:(k + 1) * 256],
                                  start=(j == 0 and k == 0), stop=(j == 3 and k == 3))
                    last.then_inc(S["scores_done"], 1)
                    c.note("scores_done")

                def turn_probabilities():
                    c.take("p_scaled")
                    for m in range(2):
                        last = turn(bank(SCORE_SLOT, 1, m * P, (m + 1) * P), p_dec[:, m * P:(m + 1) * P])
                    last.then_inc(S["p_turned"], 1)
                    c.note("p_turned")

                def output():
                    c.take("p_placed")
                    for b in range(2):
                        c.take(f"raw_full{b}", 16)
                        for hd in range(NH):
                            e = b * NH + hd
                            for m in range(2):
                                last = mm(bank(OUT_SLOT, 1, 0, 256), pblk[:, m * 1024 + e * P:m * 1024 + (e + 1) * P],
                                          raw[:, b, m * D + hd * 256:m * D + (hd + 1) * 256],
                                          start=(e == 0 and m == 0), stop=(e == 7 and m == 1))
                        last.then_inc(S["raw_used"], 1)
                        c.note("raw_used")

                def turn_output():
                    c.take("o_copied")
                    for i in range(2):
                        last = turn(bank(OUT_SLOT, 0, i * P, (i + 1) * P), o_dec[:, i * P:(i + 1) * P])
                    last.then_inc(S["o_turned"], 1)
                    c.note("o_turned")

                c.n["raw_full0"] = c.n["raw_full1"] = 30 * 16
                turn_keys(0)
                turn_keys(1)
                c.take("q_placed")
                pe.wait_ge(S["item_done"], done_value(l, I + A_PV[3]))
                score(0)
                turn_keys(2)
                score(1)
                turn_keys(3)
                score(2)
                score(3)
                with c.loop(0, 3, GROW_PAIR) as n:
                    turn_keys(0)
                    turn_keys(1)
                    c.take("q_placed")
                    c.take("dec_exp")
                    score(0)
                    turn_keys(2)
                    score(1)
                    turn_keys(3)
                    turn_probabilities()
                    score(2)
                    score(3)
                    output()
                    turn_output()
                turn_probabilities()
                output()
                c.note("dec_exp")
                c.n["raw_full0"] = c.n["raw_full1"] = 56 * 16
                c.take("item_done")
                c.take("w_ready")
                s = slot_of(I + A_WO)
                for b in range(2):
                    if b == 1:
                        turn_output()
                        c.take("o_placed", 4)
                    for k in range(KC):
                        last = three_passes([bank(s, b, 0, HT)], k, KC, lambda a, o: w_half(a, H_WO)[:, k, :],
                                            lambda a, o: H[:, a, k, b * HT:(b + 1) * HT])
                last.then_inc(S["item_ready"], 1)
                c.note("item_ready")
                for m in range(1, 4):
                    token_item(I + A_WO + m, H_WO + m, H)
                four(I + A_WO + 4, H_WO + 4, H)
                ffn(1)

            c.take("item_done", 4)
            for t in range(5):
                if t == 3:
                    c.take("sq_added", 7)
                    for i in range(5):
                        last = mm(bank(3, 0, i, i + 1), sqsum[:, i * P:(i + 1) * P], onesd[:, 0:1], start=True,
                                  stop=True)
                    last.then_inc(S["ms_made"], 1)
                    pe.wait_ge(S["ms_read"], 1)
                if t == 4:
                    pe.wait_ge(S["y_made"], 1)
                for k in range(KC):
                    last = turn(slot(t % 4)[:, k * P:(k + 1) * P], xT[:, k, t * P:(t + 1) * P])
                last.then_inc(S["y_turned"], 1)


def parameter_rows(ffn_norm, mix_norm, xattn_norm, mem_norm, pool_scale, conv_w, final_norm):
    yield R_FFN, ffn_norm.rearrange("l w (m p) -> (l w m) p", p=P)
    yield R_FINAL, final_norm.rearrange("(m p) -> m p", p=P)
    for r, gains in zip(range(R_GAINS, R_PSCALE, 2 * KC), (mix_norm, xattn_norm, mem_norm)):
        yield r, gains.rearrange("l (m p) -> (l m) p", p=P)
    yield R_PSCALE, pool_scale.rearrange("l (m p) -> (l m) p", p=P)
    yield R_CONV, conv_w.rearrange("l k (j p) -> (l k j) p", p=P)


INPUTS = ["x_prompt", "x_sample", "mem_prompt", "cache_mem_k", "cache_mem_v", "state_conv", "state_pool", "ffn_norm",
          "ffn_w_in", "ffn_w_out", "mix_norm", "mix_w_in", "conv_w", "pool_w", "pool_scale", "mix_w_out",
          "xattn_norm", "mem_norm", "xattn_wq", "xattn_wkv", "xattn_wo", "final_norm"]
OUTPUTS = [(1, TP, D), (NB, 16, D), (DEPTH, 1, NMEM, NH, 256), (DEPTH, 1, NMEM, NH, 256), (DEPTH, 1, 2, DC),
           (DEPTH, 1, PS, DC), (DEPTH, NB, 2, DC), (DEPTH, NB, PS, DC)]


def kernel(**inputs):
    import numpy as np
    import concourse.bacc as bacc
    from concourse.bass_utils import run_bass_kernel_spmd

    nc = bacc.Bacc("TRN2", target_bir_lowering=False, num_devices=1)
    arrays, args = {}, []
    for name in INPUTS:
        a = np.ascontiguousarray(inputs[name])
        arrays[f"in_{name}"] = a
        args.append(nc.dram_tensor(f"in_{name}", a.shape, mybir.dt.from_np(a.dtype), kind="ExternalInput").ap())
    for i, shape in enumerate(OUTPUTS):
        args.append(nc.dram_tensor(f"out_{i}", shape, mybir.dt.float32, kind="ExternalOutput").ap())
    program(nc, *args)
    r = run_bass_kernel_spmd(nc, [arrays], core_ids=[0])
    return tuple(r.results[0][f"out_{i}"] for i in range(len(OUTPUTS)))
```
